# Optimizing a Trainium2 kernel written in Bass

```python
import jax
import jax.numpy as jnp
from jax import lax
import numpy as np
import math
import jax, jax.numpy as jnp

D_MODEL = 1024
BATCH = 1
SEQ = 256
DEPTH = 1

CTX_LEN = 256
GRID_W = 64
D_MIX = D_MODEL
RW_WIDTH = D_MIX // 2
RW_HEAD = 64
RW_HEADS = RW_WIDTH // RW_HEAD
DECAY_LORA = 64
AAA_LORA = 64
MLA_WIDTH = D_MIX - RW_WIDTH
MLA_HEADS = 8
QK_NOPE = 64
QK_ROPE = 32
QK_DIM = QK_NOPE + QK_ROPE
V_HEAD = MLA_WIDTH // MLA_HEADS
Q_LORA = 384
KV_LORA = 256
AXIS_DIM = QK_ROPE // 2
ROPE_THETA = 10000.0
Q_BLOCK = 128
NORM_EPS = 1e-6
LNX_EPS = 64e-5
ATTN_SCALE = QK_DIM ** -0.5
N_SHIFT = 3 * RW_WIDTH + 2 * DECAY_LORA + 2 * AAA_LORA
MLA_LAT = Q_LORA + KV_LORA + QK_ROPE
D_IN = N_SHIFT + RW_WIDTH + MLA_LAT + MLA_WIDTH
SPLITS = (N_SHIFT, N_SHIFT + RW_WIDTH, N_SHIFT + RW_WIDTH + MLA_LAT)


def rms_norm(x, g):
    xf = x.astype(jnp.float32)
    y = xf * lax.rsqrt(jnp.mean(xf * xf, axis=-1, keepdims=True) + NORM_EPS)
    return (y * g.astype(jnp.float32)).astype(x.dtype)

def token_shift(u, mu_prev, mu_next):
    prev = jnp.pad(u[:, :-1], ((0, 0), (1, 0), (0, 0)))
    nxt = jnp.pad(u[:, 1:], ((0, 0), (0, 1), (0, 0)))
    return u + mu_prev * (prev - u) + mu_next * (nxt - u)

def to_heads(t):
    return t.reshape(t.shape[:-1] + (RW_HEADS, RW_HEAD))

def rwkv_prep(u_shift, mu, w0, w2, a0, a2, k_k, k_a):
    us = token_shift(u_shift, mu[0], mu[1])
    r, k, v, w_in, a_in = jnp.split(
        us, [RW_WIDTH, 2 * RW_WIDTH, 3 * RW_WIDTH, 3 * RW_WIDTH + 2 * DECAY_LORA], axis=-1)
    B, L = us.shape[:2]
    w_in = w_in.reshape(B, L, 2, DECAY_LORA)
    a_in = a_in.reshape(B, L, 2, AAA_LORA)
    w_log = -jax.nn.softplus(-(w0[:, None, None, :] + jnp.einsum('blde,def->dblf', jnp.tanh(w_in), w2))) - 0.5
    decay = jnp.exp(-jnp.exp(w_log.astype(jnp.float32)))
    a = jax.nn.sigmoid(a0[:, None, None, :] + jnp.einsum('blde,def->dblf', a_in, a2))
    kkf = to_heads(k * k_k).astype(jnp.float32)
    kk = (kkf * lax.rsqrt(jnp.maximum(jnp.sum(kkf * kkf, -1, keepdims=True), 1e-24))).astype(k.dtype)
    a = to_heads(a)
    k_dir = to_heads(k)[None] * (1 + (a - 1) * to_heads(k_a))
    b_dir = kk[None] * a
    return to_heads(r), kk, to_heads(v), to_heads(decay), k_dir, b_dir

def rwkv_scan(state0, r, decay, k, v, a_neg, b, reverse, emit):
    xs = tuple(jnp.moveaxis(t.astype(jnp.float32), 1, 0) for t in (r, decay, k, v, a_neg, b))

    def step(S, inp):
        r_t, w_t, k_t, v_t, a_t, b_t = inp
        sa = jnp.einsum('bhij,bhj->bhi', S, a_t)
        S = S * w_t[:, :, None, :] + sa[..., None] * b_t[:, :, None, :] + v_t[..., None] * k_t[:, :, None, :]
        y = jnp.einsum('bhij,bhj->bhi', S, r_t) if emit else None
        return S, y

    S, ys = lax.scan(step, state0, xs, reverse=reverse)
    return S, (jnp.moveaxis(ys, 0, 1) if emit else None)

def rwkv_branch(prep, states0, r_k, lnx_g, lnx_b, gate, emit):
    r, kk, v, decay, k_dir, b_dir = prep
    S_f, y_f = rwkv_scan(states0[0], r, decay[0], k_dir[0], v, -kk, b_dir[0], False, emit)
    S_b, y_b = rwkv_scan(states0[1], r, decay[1], k_dir[1], v, -kk, b_dir[1], True, emit)
    if not emit:
        return None, (S_f, S_b)
    y = y_f + y_b
    mean = jnp.mean(y, -1, keepdims=True)
    var = jnp.mean(jnp.square(y - mean), -1, keepdims=True)
    yn = (y - mean) * lax.rsqrt(var + LNX_EPS) * to_heads(lnx_g).astype(jnp.float32) \
        + to_heads(lnx_b).astype(jnp.float32)
    bonus = jnp.sum(r * (k_dir[0] + k_dir[1]) * r_k, -1, keepdims=True) * v
    out = (yn + bonus.astype(jnp.float32)).astype(gate.dtype)
    B, L = gate.shape[:2]
    return out.reshape(B, L, RW_WIDTH) * jax.nn.silu(gate), (S_f, S_b)

def rot_half(t, cos, sin):
    t1, t2 = t[..., :AXIS_DIM // 2], t[..., AXIS_DIM // 2:]
    return jnp.concatenate([t1 * cos - t2 * sin, t1 * sin + t2 * cos], axis=-1)

def rope_axial(t, cos_r, sin_r, cos_c, sin_c):
    return jnp.concatenate([rot_half(t[..., :AXIS_DIM], cos_r, sin_r),
                            rot_half(t[..., AXIS_DIM:], cos_c, sin_c)], axis=-1)

def mla_queries(u_mla, q_g, w_uq, rot):
    B, L = u_mla.shape[:2]
    c_q = rms_norm(u_mla[..., :Q_LORA], q_g)
    q = jnp.einsum('blr,rf->blf', c_q, w_uq).reshape(B, L, MLA_HEADS, QK_DIM)
    if rot is not None:
        q = jnp.concatenate([q[..., :QK_NOPE], rope_axial(q[..., QK_NOPE:], *rot)], axis=-1)
    return q

def mla_keys_values(u_mla, kv_g, w_ukv, rot):
    B, L = u_mla.shape[:2]
    c_kv = rms_norm(u_mla[..., Q_LORA:Q_LORA + KV_LORA], kv_g)
    k_r = u_mla[..., Q_LORA + KV_LORA:][:, :, None, :]
    if rot is not None:
        k_r = rope_axial(k_r, *rot)
    kv = jnp.einsum('blr,rf->blf', c_kv, w_ukv).reshape(B, L, MLA_HEADS, QK_NOPE + V_HEAD)
    k_nope, v = kv[..., :QK_NOPE], kv[..., QK_NOPE:]
    k = jnp.concatenate([k_nope, jnp.broadcast_to(k_r, (B, L, MLA_HEADS, QK_ROPE))], axis=-1)
    return k, v

def softmax_attend(q, k, v):
    s = jnp.einsum('bqhd,bkhd->bhqk', q, k).astype(jnp.float32) * ATTN_SCALE
    p = jax.nn.softmax(s, axis=-1).astype(v.dtype)
    return jnp.einsum('bhqk,bkhd->bqhd', p, v)

def block_attention(q, k_all, v_all):
    B, L, H, dk = q.shape
    nb = L // Q_BLOCK
    qb = q.reshape(B, nb, Q_BLOCK, H, dk).swapaxes(0, 1)
    o = lax.map(lambda blk: softmax_attend(blk, k_all, v_all), qb)
    return o.swapaxes(0, 1).reshape(B, L, H * V_HEAD)

def hybrid_layer(x, ctx, mod, mod_c, rot, params, need_ctx_out):
    (norm_g, w_in, shift_mu, rw_w0, rw_w2, rw_a0, rw_a2, rw_kk, rw_ka, rw_rk,
     rw_lnx_g, rw_lnx_b, q_g, kv_g, w_uq, w_ukv, w_out) = params
    B, L = x.shape[:2]
    shift, scale, gate = jnp.split(mod, 3, axis=-1)
    shift_c, scale_c, gate_c = jnp.split(mod_c, 3, axis=-1)
    h = rms_norm(x, norm_g) * (1 + scale) + shift
    hc = rms_norm(ctx, norm_g) * (1 + scale_c) + shift_c
    u_sh, g_rw, u_mla, g_mla = jnp.split(h @ w_in, SPLITS, axis=-1)
    uc_sh, gc_rw, uc_mla, gc_mla = jnp.split(hc @ w_in, SPLITS, axis=-1)

    rw_p = (shift_mu, rw_w0, rw_w2, rw_a0, rw_a2, rw_kk, rw_ka)
    S0 = jnp.zeros((B, RW_HEADS, RW_HEAD, RW_HEAD), jnp.float32)
    rw_c, ctx_states = rwkv_branch(rwkv_prep(uc_sh, *rw_p), (S0, S0), rw_rk, rw_lnx_g, rw_lnx_b,
                                   gc_rw, need_ctx_out)
    rw_l, _ = rwkv_branch(rwkv_prep(u_sh, *rw_p), ctx_states, rw_rk, rw_lnx_g, rw_lnx_b, g_rw, True)

    kc, vc = mla_keys_values(uc_mla, kv_g, w_ukv, None)
    k, v = mla_keys_values(u_mla, kv_g, w_ukv, rot)
    q = mla_queries(u_mla, q_g, w_uq, rot)
    o = block_attention(q, jnp.concatenate([k, kc], axis=1), jnp.concatenate([v, vc], axis=1))
    mla_l = o * jax.nn.silu(g_mla)

    x = x + gate * (jnp.concatenate([rw_l, mla_l], axis=-1) @ w_out)
    if need_ctx_out:
        qc = mla_queries(uc_mla, q_g, w_uq, None)
        mla_c = softmax_attend(qc, kc, vc).reshape(B, ctx.shape[1], MLA_WIDTH) * jax.nn.silu(gc_mla)
        ctx = ctx + gate_c * (jnp.concatenate([rw_c, mla_c], axis=-1) @ w_out)
    return x, ctx

def first_inputs(seed: int = 0) -> dict:
    key = jax.random.key(seed)
    ks = jax.random.split(key, 24)
    f32 = jnp.float32

    def nrm(k, shape, s):
        return jax.random.normal(k, shape, f32) * s

    return {
        'x': nrm(ks[0], (BATCH, SEQ, D_MODEL), 1.0),
        'c': nrm(ks[1], (BATCH, D_MODEL), 1.0),
        'ctx': nrm(ks[2], (BATCH, CTX_LEN, D_MODEL), 1.0),
        'c_ctx': nrm(ks[3], (D_MODEL,), 1.0),
        'ada_w': nrm(ks[4], (DEPTH, D_MODEL, 3 * D_MODEL), 0.5 * D_MODEL ** -0.5),
        'ada_b': nrm(ks[5], (DEPTH, 3 * D_MODEL), 0.02),
        'norm_g': 1.0 + nrm(ks[6], (DEPTH, D_MODEL), 0.05),
        'w_in': nrm(ks[7], (DEPTH, D_MODEL, D_IN), D_MODEL ** -0.5),
        'shift_mu': jax.random.uniform(ks[8], (DEPTH, 2, N_SHIFT), f32, 0.0, 0.5),
        'rw_w0': jax.random.uniform(ks[9], (DEPTH, 2, RW_WIDTH), f32, -6.5, -1.5),
        'rw_w2': nrm(ks[10], (DEPTH, 2, DECAY_LORA, RW_WIDTH), 0.1 * DECAY_LORA ** -0.5),
        'rw_a0': nrm(ks[11], (DEPTH, 2, RW_WIDTH), 0.1),
        'rw_a2': nrm(ks[12], (DEPTH, 2, AAA_LORA, RW_WIDTH), AAA_LORA ** -0.5),
        'rw_kk': 0.85 + nrm(ks[13], (DEPTH, RW_WIDTH), 0.02),
        'rw_ka': 1.0 + nrm(ks[14], (DEPTH, RW_WIDTH), 0.02),
        'rw_rk': nrm(ks[15], (DEPTH, RW_HEADS, RW_HEAD), 0.1),
        'rw_lnx_g': 1.0 + nrm(ks[16], (DEPTH, RW_WIDTH), 0.05),
        'rw_lnx_b': nrm(ks[17], (DEPTH, RW_WIDTH), 0.02),
        'mla_q_norm_g': 1.0 + nrm(ks[18], (DEPTH, Q_LORA), 0.05),
        'mla_kv_norm_g': 1.0 + nrm(ks[19], (DEPTH, KV_LORA), 0.05),
        'mla_w_uq': nrm(ks[20], (DEPTH, Q_LORA, MLA_HEADS * QK_DIM), Q_LORA ** -0.5),
        'mla_w_ukv': nrm(ks[21], (DEPTH, KV_LORA, MLA_HEADS * (QK_NOPE + V_HEAD)), KV_LORA ** -0.5),
        'w_out': nrm(ks[22], (DEPTH, D_MIX, D_MODEL), D_MIX ** -0.5),
        'final_g': 1.0 + nrm(ks[23], (D_MODEL,), 0.05),
    }

def first_block(x, c, ctx, c_ctx, ada_w, ada_b, norm_g, w_in, shift_mu, rw_w0, rw_w2, rw_a0, rw_a2,
              rw_kk, rw_ka, rw_rk, rw_lnx_g, rw_lnx_b, mla_q_norm_g, mla_kv_norm_g, mla_w_uq,
              mla_w_ukv, w_out, final_g):
    L = x.shape[1]
    rows = L // GRID_W
    row = jnp.repeat(jnp.arange(rows, dtype=jnp.float32), GRID_W)
    col = jnp.tile(jnp.arange(GRID_W, dtype=jnp.float32), rows)
    inv_freq = ROPE_THETA ** (-jnp.arange(0, AXIS_DIM, 2, dtype=jnp.float32) / AXIS_DIM)
    ang_r = (row[:, None] * inv_freq)[:, None, :]
    ang_c = (col[:, None] * inv_freq)[:, None, :]
    rot = (jnp.cos(ang_r).astype(x.dtype), jnp.sin(ang_r).astype(x.dtype),
           jnp.cos(ang_c).astype(x.dtype), jnp.sin(ang_c).astype(x.dtype))

    for i in range(DEPTH):
        mod = (jax.nn.silu(c) @ ada_w[i] + ada_b[i])[:, None, :]
        mod_c = jax.nn.silu(c_ctx) @ ada_w[i] + ada_b[i]
        params = (norm_g[i], w_in[i], shift_mu[i], rw_w0[i], rw_w2[i], rw_a0[i], rw_a2[i], rw_kk[i],
                  rw_ka[i], rw_rk[i], rw_lnx_g[i], rw_lnx_b[i], mla_q_norm_g[i], mla_kv_norm_g[i],
                  mla_w_uq[i], mla_w_ukv[i], w_out[i])
        x, ctx = hybrid_layer(x, ctx, mod, mod_c, rot, params, i < DEPTH - 1)
    return rms_norm(x, final_g)


DEPTH_2 = 2

CHUNK = 64
SSM_WIDTH = D_MODEL // 4
SSM_GROUP = 16
SSM_GROUPS = SSM_WIDTH // SSM_GROUP
SSM_STATE = 64
GMLP_WIDTH = D_MODEL // 4
GMLP_HEADS = 4
GMLP_HEAD_DIM = GMLP_WIDTH // GMLP_HEADS
GMLP_WINDOW = 128
DIFF_WIDTH = D_MODEL // 2
DIFF_HEADS = 4
DIFF_VDIM = DIFF_WIDTH // DIFF_HEADS
DIFF_QK_DIM = DIFF_VDIM // 2
MIX_WIDTH = SSM_WIDTH + GMLP_WIDTH + DIFF_WIDTH
IN_COLS = SSM_WIDTH + 2 * GMLP_WIDTH + 3 * DIFF_WIDTH
D_FF = ((8 * D_MODEL // 3 + 127) // 128) * 128
CONV_WIDTH = 3
EPS = 1e-6


def rms_norm_2(x, g):
    xf = x.astype(jnp.float32)
    y = xf * lax.rsqrt(jnp.mean(xf * xf, axis=-1, keepdims=True) + EPS)
    return (y * g.astype(jnp.float32)).astype(x.dtype)

def rope_tables(seq):
    half = DIFF_QK_DIM // 2
    inv = ROPE_THETA ** (-jnp.arange(half, dtype=jnp.float32) / half)
    ang = jnp.arange(seq, dtype=jnp.float32)[:, None] * inv[None, :]
    ang = jnp.concatenate([ang, ang], axis=-1)
    return jnp.cos(ang), jnp.sin(ang)

def apply_rope(x, cos, sin):
    x1, x2 = jnp.split(x, 2, axis=-1)
    rot = jnp.concatenate([-x2, x1], axis=-1)
    c = cos[None, :, None, None, :]
    s = sin[None, :, None, None, :]
    return (x.astype(jnp.float32) * c + rot.astype(jnp.float32) * s).astype(x.dtype)

def s5_mixer(u, a_re, a_im, log_dt, b_re, b_im, c_re, c_im, d_skip, w_glu, b_glu):
    bsz, seq, _ = u.shape
    uf = u.astype(jnp.float32).reshape(bsz, seq, SSM_GROUPS, SSM_GROUP)
    lam = lax.complex(a_re.astype(jnp.float32), a_im.astype(jnp.float32))
    dt = jnp.exp(log_dt.astype(jnp.float32))[:, None]
    a_bar = jnp.exp(lam * dt)
    b_mat = lax.complex(b_re.astype(jnp.float32), b_im.astype(jnp.float32))
    b_bar = ((a_bar - 1.0) / lam)[..., None] * b_mat
    bu = jnp.einsum("bsgh,gph->bsgp", uf.astype(jnp.complex64), b_bar)

    def combine(left, right):
        a_l, b_l = left
        a_r, b_r = right
        return a_l * a_r, a_r * b_l + b_r

    a_seq = jnp.broadcast_to(a_bar, (1, seq) + a_bar.shape)
    _, states = lax.associative_scan(combine, (a_seq, bu), axis=1)
    c_mat = lax.complex(c_re.astype(jnp.float32), c_im.astype(jnp.float32))
    y = jnp.real(jnp.einsum("bsgp,ghp->bsgh", states, c_mat))
    y = y + d_skip.astype(jnp.float32).reshape(SSM_GROUPS, SSM_GROUP) * uf
    y = jax.nn.gelu(y.reshape(bsz, seq, SSM_WIDTH))
    y = y * jax.nn.sigmoid(y @ w_glu.astype(jnp.float32) + b_glu.astype(jnp.float32))
    return y.astype(u.dtype)

def spatial_gating(u, v, v_gain, w_s, b_s):
    bsz, seq, _ = u.shape
    v = rms_norm_2(v, v_gain)
    nwin = seq // GMLP_WINDOW
    v = v.reshape(bsz, nwin, GMLP_WINDOW, GMLP_HEADS, GMLP_HEAD_DIM)
    pos_chunk = jnp.arange(GMLP_WINDOW) // CHUNK
    mask = pos_chunk[None, :] <= pos_chunk[:, None]
    w = jnp.where(mask[None], w_s, 0).astype(v.dtype)
    mixed = jnp.einsum("hij,bnjhc->bnihc", w, v)
    mixed = mixed + b_s.astype(v.dtype).T[None, None, :, :, None]
    return u * mixed.reshape(bsz, seq, GMLP_WIDTH)

def diff_attention(q, k, v, q_gain, k_gain, lam_q1, lam_k1, lam_q2, lam_k2, sub_gain, lambda_init):
    bsz, seq, _ = q.shape
    q = q.reshape(bsz, seq, DIFF_HEADS, 2, DIFF_QK_DIM)
    k = k.reshape(bsz, seq, DIFF_HEADS, 2, DIFF_QK_DIM)
    v = v.reshape(bsz, seq, DIFF_HEADS, DIFF_VDIM)
    q = rms_norm_2(q, q_gain)
    k = rms_norm_2(k, k_gain)
    cos, sin = rope_tables(seq)
    q = apply_rope(q, cos, sin)
    k = apply_rope(k, cos, sin)
    lam = (jnp.exp(jnp.sum(lam_q1.astype(jnp.float32) * lam_k1.astype(jnp.float32)))
           - jnp.exp(jnp.sum(lam_q2.astype(jnp.float32) * lam_k2.astype(jnp.float32)))
           + lambda_init)
    nblk = seq // Q_BLOCK
    q_blocks = jnp.moveaxis(q.reshape(bsz, nblk, Q_BLOCK, DIFF_HEADS, 2, DIFF_QK_DIM), 1, 0)
    key_chunk = jnp.arange(seq) // CHUNK
    scale = DIFF_QK_DIM ** -0.5

    def block(args):
        qb, blk = args
        q_chunk = (blk * Q_BLOCK + jnp.arange(Q_BLOCK)) // CHUNK
        mask = key_chunk[None, :] <= q_chunk[:, None]
        s = jnp.einsum("bqhcd,bkhcd->bhcqk", qb, k).astype(jnp.float32) * scale
        s = jnp.where(mask, s, -jnp.inf)
        p = jax.nn.softmax(s, axis=-1)
        w = (p[:, :, 0] - lam * p[:, :, 1]).astype(v.dtype)
        return jnp.einsum("bhqk,bkhe->bqhe", w, v)

    out = lax.map(block, (q_blocks, jnp.arange(nblk)))
    out = jnp.moveaxis(out, 0, 1).reshape(bsz, seq, DIFF_HEADS, DIFF_VDIM)
    out = rms_norm_2(out, sub_gain) * (1.0 - lambda_init)
    return out.reshape(bsz, seq, DIFF_WIDTH)

def conv_gated_mlp(x, w_up, conv_w, conv_b, w_down):
    seq = x.shape[1]
    h = x @ w_up
    hp = jnp.pad(h, ((0, 0), (CONV_WIDTH - 1, 0), (0, 0)))
    acc = conv_b
    for i in range(CONV_WIDTH):
        acc = acc + conv_w[i] * hp[:, i:i + seq]
    gate, val = jnp.split(acc, 2, axis=-1)
    return (jax.nn.gelu(gate) * val) @ w_down

def second_inputs(seed: int = 0) -> dict:
    key = jax.random.key(seed)
    ks = iter(jax.random.split(key, 40))

    def nrm(shape, std):
        return jax.random.normal(next(ks), shape, jnp.float32) * std

    L, G, P, C = DEPTH_2, SSM_GROUPS, SSM_STATE, SSM_GROUP
    x = nrm((BATCH, SEQ, D_MODEL), 1.0)
    attn_norm_g = 1.0 + nrm((L, D_MODEL), 0.02)
    w_in = nrm((L, D_MODEL, IN_COLS), D_MODEL ** -0.5)
    ssm_a_re = -0.5 + nrm((L, G, P), 0.01)
    ssm_a_im = jnp.pi * jnp.arange(P, dtype=jnp.float32)[None, None, :] + nrm((L, G, P), 0.01)
    ssm_log_dt = jax.random.uniform(next(ks), (L, G), jnp.float32, math.log(1e-3), math.log(1e-1))
    ssm_b_re = nrm((L, G, P, C), (2 * C) ** -0.5)
    ssm_b_im = nrm((L, G, P, C), (2 * C) ** -0.5)
    ssm_c_re = nrm((L, G, C, P), P ** -0.5)
    ssm_c_im = nrm((L, G, C, P), P ** -0.5)
    ssm_d = nrm((L, SSM_WIDTH), 1.0)
    ssm_w_glu = nrm((L, SSM_WIDTH, SSM_WIDTH), SSM_WIDTH ** -0.5)
    ssm_b_glu = nrm((L, SSM_WIDTH), 0.02)
    gmlp_v_g = 1.0 + nrm((L, GMLP_WIDTH), 0.02)
    gmlp_w_s = nrm((L, GMLP_HEADS, GMLP_WINDOW, GMLP_WINDOW), GMLP_WINDOW ** -0.5)
    gmlp_b_s = 1.0 + nrm((L, GMLP_HEADS, GMLP_WINDOW), 0.02)
    q_norm_g = 1.0 + nrm((L, DIFF_QK_DIM), 0.02)
    k_norm_g = 1.0 + nrm((L, DIFF_QK_DIM), 0.02)
    lambda_q1 = nrm((L, DIFF_QK_DIM), 0.1)
    lambda_k1 = nrm((L, DIFF_QK_DIM), 0.1)
    lambda_q2 = nrm((L, DIFF_QK_DIM), 0.1)
    lambda_k2 = nrm((L, DIFF_QK_DIM), 0.1)
    subln_g = 1.0 + nrm((L, DIFF_VDIM), 0.02)
    w_out = nrm((L, MIX_WIDTH, D_MODEL), MIX_WIDTH ** -0.5)
    ffn_norm_g = 1.0 + nrm((L, D_MODEL), 0.02)
    w_up = nrm((L, D_MODEL, 2 * D_FF), D_MODEL ** -0.5)
    conv_w = nrm((L, CONV_WIDTH, 2 * D_FF), CONV_WIDTH ** -0.5)
    conv_b = nrm((L, 2 * D_FF), 0.02)
    w_down = nrm((L, D_FF, D_MODEL), D_FF ** -0.5)
    return {"x": x, "attn_norm_g": attn_norm_g, "w_in": w_in,
            "ssm_a_re": ssm_a_re, "ssm_a_im": ssm_a_im, "ssm_log_dt": ssm_log_dt,
            "ssm_b_re": ssm_b_re, "ssm_b_im": ssm_b_im, "ssm_c_re": ssm_c_re, "ssm_c_im": ssm_c_im,
            "ssm_d": ssm_d, "ssm_w_glu": ssm_w_glu, "ssm_b_glu": ssm_b_glu,
            "gmlp_v_g": gmlp_v_g, "gmlp_w_s": gmlp_w_s, "gmlp_b_s": gmlp_b_s,
            "q_norm_g": q_norm_g, "k_norm_g": k_norm_g,
            "lambda_q1": lambda_q1, "lambda_k1": lambda_k1, "lambda_q2": lambda_q2, "lambda_k2": lambda_k2,
            "subln_g": subln_g, "w_out": w_out, "ffn_norm_g": ffn_norm_g,
            "w_up": w_up, "conv_w": conv_w, "conv_b": conv_b, "w_down": w_down}

def second_block(x, attn_norm_g, w_in, ssm_a_re, ssm_a_im, ssm_log_dt, ssm_b_re, ssm_b_im,
              ssm_c_re, ssm_c_im, ssm_d, ssm_w_glu, ssm_b_glu, gmlp_v_g, gmlp_w_s, gmlp_b_s,
              q_norm_g, k_norm_g, lambda_q1, lambda_k1, lambda_q2, lambda_k2, subln_g, w_out,
              ffn_norm_g, w_up, conv_w, conv_b, w_down):
    o1 = SSM_WIDTH
    o2 = o1 + GMLP_WIDTH
    o3 = o2 + GMLP_WIDTH
    o4 = o3 + DIFF_WIDTH
    o5 = o4 + DIFF_WIDTH
    h = x
    for layer in range(DEPTH_2):
        lambda_init = 0.8 - 0.6 * math.exp(-0.3 * layer)
        xn = rms_norm_2(h, attn_norm_g[layer])
        proj = xn @ w_in[layer]
        u_ssm, u_g, v_g, q, k, v = jnp.split(proj, [o1, o2, o3, o4, o5], axis=-1)
        y_ssm = s5_mixer(u_ssm, ssm_a_re[layer], ssm_a_im[layer], ssm_log_dt[layer],
                         ssm_b_re[layer], ssm_b_im[layer], ssm_c_re[layer], ssm_c_im[layer],
                         ssm_d[layer], ssm_w_glu[layer], ssm_b_glu[layer])
        y_sgu = spatial_gating(u_g, v_g, gmlp_v_g[layer], gmlp_w_s[layer], gmlp_b_s[layer])
        y_diff = diff_attention(q, k, v, q_norm_g[layer], k_norm_g[layer],
                                lambda_q1[layer], lambda_k1[layer], lambda_q2[layer], lambda_k2[layer],
                                subln_g[layer], lambda_init)
        mixed = jnp.concatenate([y_ssm, y_sgu, y_diff], axis=-1)
        h = h + mixed @ w_out[layer]
        xn = rms_norm_2(h, ffn_norm_g[layer])
        h = h + conv_gated_mlp(xn, w_up[layer], conv_w[layer], conv_b[layer], w_down[layer])
    return h


def setup_inputs(seed=0):
    out = dict(first_inputs(seed))
    for name, value in second_inputs(seed + 1).items():
        if name != "x":
            out[name + "_2"] = value
    return out


def reference(
    x, c, ctx, c_ctx, ada_w, ada_b, norm_g, w_in, shift_mu, rw_w0, rw_w2, rw_a0, rw_a2, rw_kk,
    rw_ka, rw_rk, rw_lnx_g, rw_lnx_b, mla_q_norm_g, mla_kv_norm_g, mla_w_uq, mla_w_ukv, w_out,
    final_g, attn_norm_g_2, w_in_2, ssm_a_re_2, ssm_a_im_2, ssm_log_dt_2, ssm_b_re_2,
    ssm_b_im_2, ssm_c_re_2, ssm_c_im_2, ssm_d_2, ssm_w_glu_2, ssm_b_glu_2, gmlp_v_g_2,
    gmlp_w_s_2, gmlp_b_s_2, q_norm_g_2, k_norm_g_2, lambda_q1_2, lambda_k1_2, lambda_q2_2,
    lambda_k2_2, subln_g_2, w_out_2, ffn_norm_g_2, w_up_2, conv_w_2, conv_b_2, w_down_2,
):
    x = first_block(
        x, c, ctx, c_ctx, ada_w, ada_b, norm_g, w_in, shift_mu, rw_w0, rw_w2, rw_a0, rw_a2,
        rw_kk, rw_ka, rw_rk, rw_lnx_g, rw_lnx_b, mla_q_norm_g, mla_kv_norm_g, mla_w_uq,
        mla_w_ukv, w_out, final_g,
    )
    return second_block(
        x, attn_norm_g_2, w_in_2, ssm_a_re_2, ssm_a_im_2, ssm_log_dt_2, ssm_b_re_2, ssm_b_im_2,
        ssm_c_re_2, ssm_c_im_2, ssm_d_2, ssm_w_glu_2, ssm_b_glu_2, gmlp_v_g_2, gmlp_w_s_2,
        gmlp_b_s_2, q_norm_g_2, k_norm_g_2, lambda_q1_2, lambda_k1_2, lambda_q2_2, lambda_k2_2,
        subln_g_2, w_out_2, ffn_norm_g_2, w_up_2, conv_w_2, conv_b_2, w_down_2,
    )


_drawn_inputs = setup_inputs


def setup_inputs(seed=0):
    import zlib

    import numpy as np

    out = dict(_drawn_inputs(seed))
    spreads = {}
    factors = {'rw_w2': 8.0,
     'rw_a0': 7.277,
     'rw_kk': 5.737,
     'rw_ka': 6.059,
     'rw_lnx_g': 4.962,
     'rw_lnx_b': 8.0,
     'mla_q_norm_g': 8.0,
     'mla_kv_norm_g': 8.0,
     'mla_w_uq': 2.908,
     'ssm_a_re_2': 64.0,
     'ssm_a_im_2': 29.216,
     'ssm_log_dt_2': 29.504,
     'ssm_b_re_2': 40.856,
     'ssm_b_im_2': 43.128,
     'ssm_c_re_2': 40.608,
     'ssm_c_im_2': 41.2,
     'ssm_b_glu_2': 43.393,
     'gmlp_v_g_2': 5.746,
     'gmlp_b_s_2': 5.228,
     'q_norm_g_2': 4.509,
     'k_norm_g_2': 4.938,
     'subln_g_2': 4.937,
     'ffn_norm_g_2': 3.231,
     'conv_b_2': 3.173}
    for name, (base, spread) in spreads.items():
        noise = np.random.default_rng([zlib.crc32(name.encode()), seed]).standard_normal(out[name].shape)
        drawn = base * np.exp(spread * noise) if base else spread * noise
        out[name] = jnp.asarray(drawn.astype(out[name].dtype))
    for name, factor in factors.items():
        out[name] = (out[name] * factor).astype(out[name].dtype)
    return out
```

```python
from contextlib import ExitStack
from itertools import count as count_from
import math

import numpy as np

import concourse.bass as bass
from concourse import mybir

ALU = mybir.AluOpType
ACT = mybir.ActivationFunctionType
F32 = mybir.dt.float32
U8 = mybir.dt.uint8
AX_X = mybir.AxisListType.X
MUL, ADD, SUB, MAX, POW = ALU.mult, ALU.add, ALU.subtract, ALU.max, ALU.pow

P = 128
D = 1024
SEQ = 256
KD = D // P
RW, HEAD, HEADS = 512, 64, 8
RB = RW // P
N_SHIFT = 3 * RW + 256
Q_LORA, KV_LORA, ROPE = 384, 256, 32
QK = 96
ATTN_SCALE = QK ** -0.5
LNX_EPS = 64e-5
EPS = 1e-6
DECAY = math.exp(-0.5)
DEPTH = 2
SSM, GROUPS, STATE = 256, 16, 64
ST = GROUPS * STATE // P
D_FF = 2816
FB = D_FF // P
PAIRS = 2
UP_TILES = FB // PAIRS
DOWN_K = 4
DOWN_TILES = -(-FB // DOWN_K)
RING_1, RING_2 = 3, 4
SLOT = KD * 512
TWO_PI = 2.0 * math.pi
TWO_PI_DOWN = 6.2831845
ROUND = 1.5 * 2.0 ** 23
PI_PARTS = (6.28125, 0.0019350051879882812, TWO_PI - 6.28125 - 0.0019350051879882812)
GELU_C = math.sqrt(2.0 / math.pi)
P2_DMAS = 23

COLS_1, COLS_2A, COLS_2B = {}, {}, {}
for table, rows in ((COLS_1, (("norm_g", 8), ("mu_prev", 14), ("mu_next", 14), ("w0", 8), ("a0", 8), ("kk", 4), ("ka", 4),
                              ("rk", 4), ("lnx_g", 4), ("lnx_b", 4), ("q_g", 3), ("kv_g", 2), ("ada_b", 24))),
                    (COLS_2A, (("conv01", 88), ("attn_g", 8), ("ffn_g", 8), ("ssm_d", 2), ("b_glu", 2), ("v_g", 2), ("sub_g", 1))),
                    (COLS_2B, (("conv2", 44), ("conv_b", 44), ("a_re", 8), ("a_im", 8)))):
    at = 0
    for name, n in rows:
        table[name] = at
        at += n
    table["all"] = at

CONST = {}
at = 0
for name, n in (("ident", 128), ("half_ones", 128), ("ones", 128), ("up_strict", 128), ("up_incl", 128), ("lo_strict", 128),
                ("lo_incl", 128), ("up_1", 128), ("lo_1", 128), ("cos_ax", 32), ("sin_ax", 32), ("cos_d", 64), ("sin_d", 64),
                ("time", 256), ("group_par", 128), ("state_par", 2), ("head_sel", 32), ("expand", 512), ("window", 128),
                ("late", 256), ("negpow", 1)):
    CONST[name] = at
    at += n
N_CONST = at


def shape_constants():
    c = np.zeros((P, N_CONST), np.float32)
    i = np.arange(P)

    def put(name, a):
        c[:a.shape[0], CONST[name]:CONST[name] + a.shape[1]] = a
    put("ident", np.eye(P))
    put("half_ones", (i[:, None] // 64 == i[None, :] // 64).astype(np.float32))
    put("ones", np.ones((P, P)))
    put("up_strict", (i[:, None] < i[None, :]).astype(np.float32))
    put("up_incl", (i[:, None] <= i[None, :]).astype(np.float32))
    put("lo_strict", (i[:, None] > i[None, :]).astype(np.float32))
    put("lo_incl", (i[:, None] >= i[None, :]).astype(np.float32))
    low = {b: ((i[:, None] // (2 * b) == i[None, :] // (2 * b)) & (i[:, None] // b > i[None, :] // b)) for b in (1, 2, 4, 8, 16, 32, 64)}
    put("lo_1", low[1].astype(np.float32))
    put("up_1", low[1].T.astype(np.float32))
    tok = np.arange(SEQ)
    inv = (np.float32(10000.0) ** (-np.arange(0, 16, 2, dtype=np.float32) / np.float32(16))).astype(np.float32)
    ang = np.stack([(tok // 64).astype(np.float32)[:, None] * inv, (tok % 64).astype(np.float32)[:, None] * inv], 1)
    put("cos_ax", np.cos(ang).reshape(2, P, 16).transpose(1, 0, 2).reshape(P, 32))
    put("sin_ax", np.sin(ang).reshape(2, P, 16).transpose(1, 0, 2).reshape(P, 32))
    inv = (np.float32(10000.0) ** (-np.arange(32, dtype=np.float32) / np.float32(32))).astype(np.float32)
    ang = tok.astype(np.float32)[:, None] * inv
    put("cos_d", np.cos(ang).reshape(2, P, 32).transpose(1, 0, 2).reshape(P, 64))
    put("sin_d", np.sin(ang).reshape(2, P, 32).transpose(1, 0, 2).reshape(P, 64))
    put("time", np.tile(np.arange(256, dtype=np.float32), (P, 1)))
    put("group_par", ((i[:, None] // 16) % 2 == i[None, :] // 64).astype(np.float32))
    put("state_par", (i[:, None] // 64 == np.arange(2)[None, :]).astype(np.float32))
    sel = np.zeros((P, RB, 8), np.float32)
    for b in range(RB):
        for h in range(2):
            sel[64 * h:64 * h + 64, b, 2 * b + h] = 1
    put("head_sel", sel.reshape(P, 32))
    put("expand", sel.transpose(2, 1, 0).reshape(8, 512))
    put("window", (i[:, None] // 64 <= i[None, :] // 64).astype(np.float32))
    late = np.zeros((1, 256), np.float32)
    late[0, 0:64] = 1.0
    late[0, 192:256] = -1e30
    put("late", late)
    put("negpow", np.full((P, 1), -0.5))
    levels = np.stack([low[b] for b in (2, 4, 8, 16, 32, 64)] + [low[b].T for b in (2, 4, 8, 16, 32, 64)], 1)
    return c, np.ascontiguousarray(levels.reshape(P, 12 * P).astype(np.float32))


def weight_tiles(w):
    tiles = []

    def add(name, src, k, cols):
        s = src.rearrange("(k p) n -> p k n", p=P)
        half = (k + 1) // 2
        tiles.append((name, [((0, half * cols), (half, cols), s[:, 0:half, :]), ((half * cols, k * cols), (k - half, cols), s[:, half:k, :])]))
    for n in range(6):
        add(("ada", n), w["ada_w"][0, :, 512 * n:512 * n + 512], KD, 512)
    for n, (a, b) in enumerate(((1536, 2048), (512, 1024), (1024, 1536), (0, 512), (2048, 2560), (2560, 2976), (2976, 3488))):
        add(("in", n), w["w_in"][0, :, a:b], KD, b - a)
    add("uq", w["mla_w_uq"][0], 3, 768)
    add("ukv", w["mla_w_ukv"][0], 2, 1024)
    for n in range(2):
        add(("out", n), w["w_out"][0, :, 512 * n:512 * n + 512], KD, 512)
    fg = w["final_g"].rearrange("(o n) -> o n", o=1)
    tiles.append(("final_g", [((512 * n, 512 * n + 512), None, fg[:, 512 * n:512 * n + 512].to_broadcast([P, 512])) for n in range(2)]))
    for l in range(DEPTH):
        for n, (a, b) in enumerate(((0, 512), (512, 768), (768, 1280), (1280, 1792), (1792, 2304))):
            add(("in2", l, n), w["w_in_2"][l, :, a:b], KD, b - a)
        for n in range(2):
            add(("out2", l, n), w["w_out_2"][l, :, 512 * n:512 * n + 512], KD, 512)
        for n in range(UP_TILES):
            parts = []
            for half in range(2):
                c0 = half * D_FF + n * PAIRS * P
                parts.append(((half * KD * 256, (half + 1) * KD * 256), (KD, 256),
                              w["w_up_2"][l, :, c0:c0 + PAIRS * P].rearrange("(k p) n -> p k n", p=P)))
            tiles.append((("up", l, n), parts))
        for n in range(DOWN_TILES):
            k = min(DOWN_K, FB - n * DOWN_K)
            add(("down", l, n), w["w_down_2"][l, n * DOWN_K * P:(n * DOWN_K + k) * P, :], k, 1024)
    return tiles

PROJ = [[("w", 0, 0, 128, 512), ("a", 0, 128, 128, 512), ("g", 0, 256, 128, 256), ("g", 1, 384, 128, 256)],
        [("k", b, 128 * b, 128, 512) for b in range(4)],
        [("v", b, 128 * b, 128, 512) for b in range(4)],
        [("r", b, 128 * b, 128, 256) for b in range(4)],
        [("g", 2, 0, 128, 256), ("g", 3, 128, 128, 256), ("cq", 0, 256, 128, 256), ("cq", 1, 384, 128, 256)],
        [("cq", 2, 0, 128, 256), ("ckv", 0, 128, 128, 512), ("ckv", 1, 256, 128, 512), ("kr", 0, 384, 32, 512)],
        [("gm", b, 128 * b, 128, 256) for b in range(4)]]
MU_BLOCK = {"r": 0, "k": 4, "v": 8, "w": 12, "a": 13}
SHIFTED = [(k, i) for tile in PROJ for k, i, *_ in tile if k in MU_BLOCK]
GATES = [(k, i) for tile in PROJ for k, i, *_ in tile if k in ("g", "gm")]
LATENTS = [(k, i) for tile in PROJ for k, i, *_ in tile if k in ("cq", "ckv", "kr")]
US = {key: n + 1 for n, key in enumerate(SHIFTED)}
ORDER = ((2, 3, 0, 1), (3, 2, 1, 0))
LEVELS = 6

SEMAPHORES = """angle_raw a_bar_sc act_T angle b_spread bk_ch bonus_in c0 c_masked c_silu c_tanh consts crow d_bias d_hat d_rstd d_var
 d_w decays derived dt_exp e_made g_tanh gelu_in gelu_tanh h0 hp_pads k_tok kk_rn kk_sq kkf lam_exp lam_sum
 levels lora lw_in m_bias m_prob mix_gmlp mix_rw mix_ssm mod_cols out_done p2_load pads params_1 params_2 q2
 q_tok qk_rot qk_rstd qk_var rotated rotated_used rstd_1 rstd_a rstd_f rstd_lat s_in scanned sine ssq ssq_a
 ssq_f tables u_theta us var_1 var_a var_f vec_step vg_n vg_rstd vg_var weights_used x1 x_in xs xs_a y_cubic
 y_gelu y_hat y_rstd y_tanh y_var""".split()


def build(nc, w, consts, levels, out):
    tiles = weight_tiles(w)
    index = {name: n for n, (name, _) in enumerate(tiles)}
    first_2 = index[("in2", 0, 0)]
    slot_of, fills, replaces, owner, count = [], [], [], {}, {}
    for n in range(len(tiles)):
        s = n % RING_1 if n < first_2 else (n - first_2) % RING_2
        slot_of.append(s)
        count[s] = count.get(s, 0) + 1
        fills.append(count[s])
        replaces.append(owner.get(s))
        owner[s] = n

    with ExitStack() as ctx:
        def sb(name, shape, dt=F32):
            return ctx.enter_context(nc.sbuf_tensor(name, shape, dt))

        con = sb("con", [P, N_CONST])
        lev = sb("lev", [P, 12 * P], U8)
        ring = sb("ring", [P, RING_1 * SLOT])
        xc = sb("xc", [P, 4, D])
        mixT = sb("mixT", [P, 8, SEQ])
        prm = sb("prm", [P, 104])
        prm2 = sb("prm2", [P, 432])
        small = sb("small", [P, 512])
        NW = 30600
        work = sb("work", [P, NW])

        def take_work(at, *shape):
            n = int(np.prod(shape))
            assert at + n <= NW, (at, n)
            v = work[:, at:at + n]
            if len(shape) > 1:
                names = "abcd"[:len(shape)]
                v = v.rearrange(f"p ({' '.join(names)}) -> p {' '.join(names)}", **{k: m for k, m in zip(names, shape)})
            return v

        def C(name, n=P, rows=P):
            return con[0:rows, CONST[name]:CONST[name] + n]

        def col(name, n=1, i=0):
            a = COLS_1[name] + i
            return prm[:, a:a + n]

        bank = [ctx.enter_context(nc.psum_tensor(f"bank{b}", [P, 512], F32)) for b in range(8)]
        S = {n: ctx.enter_context(nc.semaphore(n)) for n in SEMAPHORES}
        bank_full = [ctx.enter_context(nc.semaphore(f"bank_full{b}")) for b in range(8)]
        bank_free = [ctx.enter_context(nc.semaphore(f"bank_free{b}")) for b in range(8)]
        slot_full = [ctx.enter_context(nc.semaphore(f"slot_full{s}")) for s in range(RING_2)]

        turns = {"short": 0, "long": 0}
        place = {}

        def turn(key, pool="short"):
            first, n = (0, 6) if pool == "short" else (6, 2)
            b, use = first + turns[pool] % n, turns[pool] // n
            turns[pool] += 1
            assert key not in place, key
            place[key] = (b, use + 1)
            return bank_free[b], use

        def bank_of(key):
            return bank[place[key][0]]

        def filling(key):
            return bank_full[place[key][0]], 1

        def when_full(key):
            return bank_full[place[key][0]], place[key][1]

        def emptying(key):
            return bank_free[place[key][0]], 1

        def when_empty(key):
            return bank_free[place[key][0]], place[key][1]

        vec_steps = count_from(1)

        def slot(n):
            s = slot_of[n]
            return ring[:, s * SLOT:(s + 1) * SLOT] if s < RING_1 else work[:, NW - (RING_2 - s) * SLOT:NW - (RING_2 - s - 1) * SLOT]

        usw, usa = take_work(0, 512), take_work(512, 512)
        kk = take_work(1024, RB, 512)
        kb = take_work(3072, RB, 512)
        vb = take_work(5120, RB, 512)
        vtok = take_work(7168, 4, 512)
        grw = take_work(9216, RB, SEQ)
        state = take_work(10240, 2, RB, 64)
        A0 = 10752
        ytok = xc[:, 2, :].rearrange("p (t n) -> p t n", t=2)
        rb = xc[:, 3, :].rearrange("p (b n) -> p b n", b=RB)
        kds = mixT[:, 0:4, :]
        lat_q, lat_kv = take_work(A0, 3, SEQ), take_work(A0 + 768, 2, 512)
        sq_q, sq_kv = take_work(A0 + 1792, 3, SEQ), take_work(A0 + 2560, 2, 512)
        krT = take_work(A0 + 3584, 512)
        kT = take_work(A0, HEADS, 512)
        gm = take_work(A0 + 4096, RB, SEQ)
        B0 = A0 + 5120
        hT = take_work(B0, KD, 512)
        junk = take_work(B0, D)
        xs = take_work(B0 + 4096, 4, D)
        sqk = take_work(B0 + 4096, RB, 512)
        rn = take_work(B0 + 10240, 512)
        ubuf = take_work(B0 + 8192, 2, 2, 258)
        gtmp = take_work(B0 + 9224, 2, SEQ)
        crow, cth = take_work(B0 + 9736, P), take_work(B0 + 9864, P)
        prow = take_work(B0 + 9992, P)
        prow2 = take_work(B0 + 10120, 4, P)
        lev_f = take_work(B0 + 10632, 12 * P)
        lora = take_work(29576, 2, 512)
        qtok = take_work(B0, 2, 768)
        ktok = take_work(B0 + 1536, 4, 768)
        vm = take_work(B0 + 4608, 4, 512)
        qT = take_work(B0 + 6656, HEADS, SEQ)
        prob = take_work(B0 + 8704, 3, 512)
        pT = take_work(B0 + 10240, 2, 512)
        rtmp = take_work(B0 + 11264, 4, P)
        krt = take_work(B0 + 11776, 4, 32)
        a_ch, r_ch = take_work(A0, 2, RB, P), take_work(A0 + 1024, 2, RB, P)
        b_ch, k_ch = take_work(A0 + 2048, RB, P), take_work(A0 + 2560, RB, P)
        b_tok, k_tok = take_work(A0 + 3072, 2, 512), take_work(A0 + 4096, 2, 512)
        QM, AK = take_work(A0 + 5120, 2, 8, P), take_work(A0 + 7168, 2, 8, P)
        RBm, RKm = take_work(A0 + 9216, 2, 8, P), take_work(A0 + 11264, 2, 8, P)
        NT = take_work(A0 + 13312, 2, 2, 4, P)
        TM, XM = take_work(A0 + 15360, 2, 4, P), take_work(A0 + 16384, 2, 4, P)
        thw, LL = take_work(A0 + 17408, RB, P), take_work(A0 + 17920, RB, P)
        tha, E0 = vb[:, :, 256:384], vb[:, :, 384:512]
        rhs_sb = XM.rearrange("p d a b -> p d (a b)")
        sa_sb = TM.rearrange("p d a b -> p d (a b)")
        bon, yn = take_work(A0 + 5120, RB, SEQ), take_work(A0 + 6144, RB, SEQ)
        ysq = take_work(A0 + 7168, 2, 512)
        gate_b = take_work(0, D)
        b_rows, c_rows = take_work(0, 2, ST, 16), take_work(256, 2, 2, P)
        ws, bs_b = take_work(768, 4, P), take_work(1280, 2, P)
        gains = take_work(1536, 4, 64)
        lam_b = take_work(1792, 4, 64)
        ldt_b = take_work(2048, 16)
        wglu = take_work(2064, 2, SEQ)
        M0 = 2576
        xnT = take_work(M0, KD, SEQ)
        uT, ug = take_work(M0 + 2048, 2, SEQ), take_work(M0 + 2560, 2, SEQ)
        vg = take_work(M0 + 3072, 2, SEQ)
        qk = take_work(M0 + 3584, 2, 2, 512)
        v2 = take_work(M0 + 5632, 2, 512)
        qkr = take_work(M0 + 6656, 2, 2, 512)
        bT = take_work(M0 + 8704, 2, 2, P)
        cT = take_work(M0 + 9216, 3, 2, P)
        wsT = take_work(M0 + 9984, 4, P)
        csc = take_work(M0 + 10496, ST, 3, SEQ)
        G0 = M0 + 16640
        m1, m2, xr = take_work(G0, 512), take_work(G0 + 512, 512), take_work(G0 + 1024, 512)
        gs = take_work(G0 + 1536, 2, 512)
        pr1, pr2 = take_work(G0 + 2560, 2, 512), take_work(G0 + 3584, 2, 512)
        qT2, kT2 = xnT[:, 0:4, :], xnT[:, 4:8, :]
        H0 = G0 + 4608
        prob2, wT2 = take_work(H0, 2, 512), take_work(H0 + 1024, 2, 512)
        o2 = qkr[:, 0]
        junk2, bexp = take_work(H0, D), take_work(H0 + 1024, 2, 2, 4, 32)
        tabs = take_work(H0 + 1536, 2, 2, 2, 64)
        xs2 = take_work(G0 + 2048, 2, D)
        rot = take_work(G0, 2, 8, 64)
        ang = take_work(G0, ST, SEQ)
        actT = take_work(M0 + 10496, FB, SEQ)
        hp = take_work(M0 + 16128, 2, 2, 258)
        cv = take_work(M0 + 17160, 2, 2, SEQ)
        ge = take_work(M0 + 18184, 2, 2, SEQ)
        assert H0 + 2048 <= NW - (RING_2 - RING_1) * SLOT

        def shift_dest(key):
            kind, i = key
            return {"w": usw, "a": usa}[kind] if kind in "wa" else {"k": kb, "v": vb, "r": rb}[kind][:, i, :]

        tb = take_work(H0, 4, ST, 16)
        vtmp = take_work(H0, 512)
        xtmp = take_work(B0 + 2048, 512)

        def k2(l, name, n=1, i=0):
            base = (COLS_2A["all"] + COLS_2B["all"]) * l
            if name in COLS_2A:
                return prm2[:, base + COLS_2A[name] + i:base + COLS_2A[name] + i + n]
            base += COLS_2A["all"]
            return prm2[:, base + COLS_2B[name] + i:base + COLS_2B[name] + i + n]

        block = ctx.enter_context(nc.Block())

        released = []

        @block.tensor
        def _(pe):
            mm, tr = nc.tensor.matmul, nc.tensor.transpose
            ident = C("ident")
            used, partly = [0], [0]

            def weights(name, *shape):
                n = index[name]
                assert n == used[0], (name, n, used[0])
                used[0] += 1
                pe.wait_ge(slot_full[slot_of[n]], 32 * fills[n])
                v = slot(n)[:, 0:int(np.prod(shape))]
                return v.rearrange("p (k n) -> p k n", k=shape[0])

            def weights_done(key=None, ins=None):
                if ins is not None:
                    ins.then_inc(S["weights_used"], 1)
                    partly[0] += 1
                released.append((bank_full[place[key][0]], place[key][1]) if ins is None else (S["weights_used"], partly[0]))

            pe.wait_ge(S["consts"], 16)
            pe.wait_ge(S["params_1"], 16 * 13)
            pe.wait_ge(*turn("prm"))
            b = bank_of("prm")
            tr(b[:, 0:COLS_1["all"]], prow[0:COLS_1["all"], :], ident[0:COLS_1["all"], 0:COLS_1["all"]]).then_inc(*filling("prm"))
            pe.wait_ge(S["c_silu"], 1)
            pe.wait_ge(*turn("ccol"))
            b = bank_of("ccol")
            tr(b[:, 0:16], crow[0:16, :], ident[0:16, 0:16]).then_inc(*filling("ccol"))
            pe.wait_ge(S["params_2"], 16 * 24)
            pe.wait_ge(*turn("prm2"))
            b = bank_of("prm2")
            at = 0
            for l in range(DEPTH):
                for n, rows in enumerate((COLS_2A["all"], COLS_2B["all"])):
                    ins = tr(b[:, at:at + rows], prow2[0:rows, 2 * l + n, :], ident[0:rows, 0:rows])
                    at += rows
            ins.then_inc(*filling("prm2"))
            pe.wait_ge(*when_empty("ccol"))
            pe.wait_ge(*turn("mod"))
            b = bank_of("mod")
            cc = small[:, 0:16].rearrange("p (j k) -> p k j", j=2)
            for n in range(6):
                wt = weights(("ada", n), KD, 512)
                for j in range(4):
                    m = 4 * n + j
                    for k in range(KD):
                        ins = mm(b[:, 2 * m:2 * m + 2], wt[:, k, P * j:P * j + P], cc[:, k, :], start=(k == 0), stop=(k == KD - 1))
                if n < 5:
                    weights_done(ins=ins)
            ins.then_inc(*filling("mod"))
            weights_done("mod")
            pe.wait_ge(S["xs"], 4)
            for k in range(KD):
                pe.wait_ge(*turn(("hT", k)))
                b = bank_of(("hT", k))
                for t in range(4):
                    ins = tr(b[:, P * t:P * t + P], xs[:, t, P * k:P * k + P], ident)
                ins.then_inc(*filling(("hT", k)))
            for k in range(KD):
                pe.wait_ge(*when_empty(("hT", k)))
            for n, blocks in enumerate(PROJ):
                width = blocks[-1][2] + blocks[-1][3]
                wt = weights(("in", n), KD, width)
                for kind, i, off, rows, toks in blocks:
                    pe.wait_ge(*turn((kind, i)))
                    b = bank_of((kind, i))
                    for k in range(KD):
                        ins = mm(b[0:rows, 0:toks], wt[:, k, off:off + rows], hT[:, k, 0:toks], start=(k == 0), stop=(k == KD - 1))
                    ins.then_inc(*filling((kind, i)))
                weights_done((kind, i))
            pe.wait_ge(*when_empty(("kr", 0)))
            pe.wait_ge(*turn("lat_ssq"))
            b = bank_of("lat_ssq")
            for c, (sq, blocks, t) in enumerate([(sq_q, 3, 0), (sq_q, 3, 1)] + [(sq_kv, 2, t) for t in range(4)]):
                for k in range(blocks):
                    ins = mm(b[:, c:c + 1], sq[:, k, P * t:P * t + P], C("ones", 1), start=(k == 0), stop=(k == blocks - 1))
            ins.then_inc(*filling("lat_ssq"))
            pe.wait_ge(*turn("krt"))
            b = bank_of("krt")
            for t in range(4):
                ins = tr(b[:, 32 * t:32 * t + 32], krT[0:32, P * t:P * t + P], ident[0:32, 0:32])
            ins.then_inc(*filling("krt"))
            pe.wait_ge(S["kk_sq"], RB)
            pe.wait_ge(*turn("kk_len"))
            b = bank_of("kk_len")
            for k in range(RB):
                ins = mm(b[0:8, :], C("head_sel", 32)[:, 8 * k:8 * k + 8], sqk[:, k, :], start=(k == 0), stop=(k == RB - 1))
            ins.then_inc(*filling("kk_len"))
            pe.wait_ge(S["us"], US[("v", 3)])
            for t in range(4):
                pe.wait_ge(*turn(("vtok", t)))
                b = bank_of(("vtok", t))
                for k in range(RB):
                    ins = tr(b[:, P * k:P * k + P], vb[:, k, P * t:P * t + P], ident)
                ins.then_inc(*filling(("vtok", t)))
            wt = weights("uq", 3, 768)
            for t in range(2):
                for j, (a, e) in enumerate(((0, 480), (480, 768))):
                    pe.wait_ge(*turn(("q", t, j)))
                    b = bank_of(("q", t, j))
                    for k in range(3):
                        ins = mm(b[:, 0:e - a], lat_q[:, k, P * t:P * t + P], wt[:, k, a:e], start=(k == 0), stop=(k == 2))
                    ins.then_inc(*filling(("q", t, j)))
            weights_done(("q", 1, 1))
            wt = weights("ukv", 2, 1024)
            for t in range(4):
                for j in range(2):
                    pe.wait_ge(*turn(("kv", t, j)))
                    b = bank_of(("kv", t, j))
                    for k in range(2):
                        ins = mm(b[:, :], lat_kv[:, k, P * t:P * t + P], wt[:, k, 512 * j:512 * j + 512], start=(k == 0), stop=(k == 1))
                    ins.then_inc(*filling(("kv", t, j)))
            weights_done(("kv", 3, 1))
            pe.wait_ge(S["kk_rn"], 1)
            for k in range(RB):
                pe.wait_ge(*turn(("kk_x", k)))
                b = bank_of(("kk_x", k))
                mm(b[:, :], C("expand", 512, 8)[:, P * k:P * k + P], rn[0:8, :], start=True, stop=True).then_inc(*filling(("kk_x", k)))
            pe.wait_ge(S["q_tok"], 2)
            for j in range(4):
                pe.wait_ge(*turn(("qT", j)))
                b = bank_of(("qT", j))
                for i in range(2):
                    for t in range(2):
                        h = 2 * j + i
                        ins = tr(b[0:QK, (2 * i + t) * P:(2 * i + t + 1) * P], qtok[:, t, QK * h:QK * h + QK], ident)
                ins.then_inc(*filling(("qT", j)))
            pe.wait_ge(S["k_tok"], 4)
            pe.wait_ge(*when_empty(("kv", 3, 1)))
            for h in range(HEADS):
                pe.wait_ge(*turn(("kT", h)))
                b = bank_of(("kT", h))
                for t in range(4):
                    ins = tr(b[0:QK, P * t:P * t + P], ktok[:, t, QK * h:QK * h + QK], ident)
                ins.then_inc(*filling(("kT", h)))
            for j in range(4):
                pe.wait_ge(*when_empty(("qT", j)))
            for h in range(HEADS):
                pe.wait_ge(*when_empty(("kT", h)))
            N = 2 * HEADS
            for i in range(N + 2):
                if i < N:
                    h, t = i // 2, i % 2
                    pe.wait_ge(*turn(("s", i)))
                    b = bank_of(("s", i))
                    mm(b[:, :], qT[0:QK, h, P * t:P * t + P], kT[0:QK, h, :], start=True, stop=True).then_inc(*filling(("s", i)))
                if 1 <= i <= N:
                    pe.wait_ge(S["m_prob"], i)
                    pe.wait_ge(*turn(("pT", i - 1)))
                    b = bank_of(("pT", i - 1))
                    for t in range(4):
                        ins = tr(b[:, P * t:P * t + P], prob[:, (i - 1) % 3, P * t:P * t + P], ident)
                    ins.then_inc(*filling(("pT", i - 1)))
                if i >= 2:
                    n = i - 2
                    h, t = n // 2, n % 2
                    pe.wait_ge(*when_empty(("pT", n)))
                    if n % 4 == 0:
                        pe.wait_ge(*turn(("o", h // 2), "long"))
                        b_o = bank_of(("o", h // 2))
                    lo = 64 * (h % 2)
                    for k in range(4):
                        ins = mm(b_o[lo:lo + 64, P * t:P * t + P], vm[:, k, 64 * h:64 * h + 64], pT[:, n % 2, P * k:P * k + P],
                                 start=(k == 0), stop=(k == 3))
                    if n % 4 == 3:
                        ins.then_inc(*filling(("o", h // 2)))
            pe.wait_ge(S["lora"], 32)
            pe.wait_ge(S["lw_in"], 1)
            pe.wait_ge(S["us"], US[("a", 0)])
            for i in range(4):
                emits = i >= 2
                for d in range(2):
                    c, n, lo = ORDER[d][i], 2 * i + d, 64 * d
                    for key, wl, src in (("lw", 0, usw), ("la", 1, usa)):
                        pe.wait_ge(*turn((key, n)))
                        b = bank_of((key, n))
                        for k in range(RB):
                            ins = mm(b[:, P * k:P * k + P], lora[lo:lo + 64, wl, P * k:P * k + P], src[lo:lo + 64, P * c:P * c + P],
                                     start=True, stop=True)
                        ins.then_inc(*filling((key, n)))
                for d in range(2):
                    n = 2 * i + d
                    pe.wait_ge(S["bk_ch"], n + 1)
                    pe.wait_ge(*turn(("bt", n)))
                    b = bank_of(("bt", n))
                    for k in range(RB):
                        ins = tr(b[:, P * k:P * k + P], b_ch[:, k, :], ident)
                    ins.then_inc(*filling(("bt", n)))
                    pe.wait_ge(*turn(("kt", n)))
                    b = bank_of(("kt", n))
                    for k in range(RB):
                        ins = tr(b[:, P * k:P * k + P], k_ch[:, k, :], ident)
                    ins.then_inc(*filling(("kt", n)))

                    def gram(key, left, right):
                        pe.wait_ge(*turn(key))
                        b = bank_of(key)
                        lo = 64 * key[2]
                        for j in range(4):
                            ins = mm(b[:, P * j:P * j + P], left[lo:lo + 64, j, :], right[lo:lo + 64, j, :], start=True, stop=True)
                        ins.then_inc(*filling(key))
                    for g in range(2):
                        gram(("nt", n, g), b_ch, a_ch[:, d])
                        gram(("ak", n, g), k_ch, a_ch[:, d])
                        if emits:
                            gram(("rb", n, g), b_ch, r_ch[:, d])
                            gram(("rk", n, g), k_ch, r_ch[:, d])
                for g in range(2):
                    for d in range(2):
                        n, m = 2 * i + d, 4 * i + 2 * g + d
                        pe.wait_ge(S["q2"], m + 1)
                        pe.wait_ge(*turn(("t2", n, g)))
                        b = bank_of(("t2", n, g))
                        for j in range(4):
                            ins = tr(b[:, P * j:P * j + P], QM[:, d, 4 * g + j, :], ident)
                        ins.then_inc(*filling(("t2", n, g)))
                    for e in range(LEVELS):
                        for d in range(2):
                            n, m = 2 * i + d, 4 * i + 2 * g + d
                            pe.wait_ge(*when_empty(("t2", n, g)))
                            if e:
                                pe.wait_ge(*when_empty(("pq", n, g, e - 1)))
                            pe.wait_ge(*turn(("x", n, g, e)))
                            b = bank_of(("x", n, g, e))
                            for j in range(4):
                                ins = mm(b[:, P * j:P * j + P], NT[:, d, g, j, :], TM[:, d, j, :], start=True, stop=True)
                            ins.then_inc(*filling(("x", n, g, e)))
                        for d in range(2):
                            n = 2 * i + d
                            pe.wait_ge(*when_empty(("x", n, g, e)))
                            if e < LEVELS - 1:
                                pe.wait_ge(*turn(("p", n, g, e)))
                                b = bank_of(("p", n, g, e))
                                for j in range(4):
                                    ins = mm(b[:, P * j:P * j + P], QM[:, d, 4 * g + j, :], XM[:, d, j, :], start=True, stop=True)
                                ins.then_inc(*filling(("p", n, g, e)))
                            pe.wait_ge(*turn(("pq", n, g, e)))
                            b = bank_of(("pq", n, g, e))
                            for j in range(4):
                                ins = mm(b[:, P * j:P * j + P], XM[:, d, j, :], QM[:, d, 4 * g + j, :], start=True, stop=True)
                            ins.then_inc(*filling(("pq", n, g, e)))
                for d in range(2):
                    n, c = 2 * i + d, ORDER[d][i]
                    for g in range(2):
                        pe.wait_ge(*when_empty(("ak", n, g)))
                    if not i:
                        for t in range(4):
                            pe.wait_ge(*when_empty(("vtok", t)))
                    if i:
                        pe.wait_ge(S["s_in"], 2 * (i - 1) + d + 1)
                    for g in range(2):
                        pe.wait_ge(*turn(("rhs", n, g)))
                        b = bank_of(("rhs", n, g))
                        lo = 64 * g
                        for j in range(4):
                            h, o = 2 * j + g, b[:, 64 * j:64 * j + 64]
                            if i:
                                mm(o, a_ch[lo:lo + 64, d, j, :], state[lo:lo + 64, d, j, :], start=True, stop=False)
                            ins = mm(o, AK[:, d, 4 * g + j, :], vtok[:, c, 64 * h:64 * h + 64], start=(i == 0), stop=True)
                        ins.then_inc(*filling(("rhs", n, g)))
                for d in range(2):
                    n = 2 * i + d
                    pe.wait_ge(*when_empty(("rhs", n, 1)))
                    for g in range(2):
                        pe.wait_ge(*when_empty(("pq", n, g, LEVELS - 1)))
                    pe.wait_ge(*turn(("sa", n)))
                    b = bank_of(("sa", n))
                    for m in range(HEADS):
                        ins = mm(b[:, 64 * m:64 * m + 64], QM[:, d, m, :], rhs_sb[:, d, 64 * m:64 * m + 64], start=True, stop=True)
                    ins.then_inc(*filling(("sa", n)))
                for d in range(2):
                    n, c = 2 * i + d, ORDER[d][i]
                    pe.wait_ge(*when_empty(("sa", n)))
                    if emits:
                        for g in range(2):
                            pe.wait_ge(*when_empty(("rb", n, g)))
                            pe.wait_ge(*when_empty(("rk", n, g)))
                        for g in range(2):
                            pe.wait_ge(*turn(("y", n, g)))
                            b = bank_of(("y", n, g))
                            lo = 64 * g
                            for j in range(4):
                                h, m, o = 2 * j + g, 4 * g + j, b[:, 64 * j:64 * j + 64]
                                mm(o, r_ch[lo:lo + 64, d, j, :], state[lo:lo + 64, d, j, :], start=True, stop=False)
                                mm(o, RBm[:, d, m, :], sa_sb[:, d, 64 * m:64 * m + 64], start=False, stop=False)
                                ins = mm(o, RKm[:, d, m, :], vtok[:, c, 64 * h:64 * h + 64], start=False, stop=True)
                            ins.then_inc(*filling(("y", n, g)))
                    if i < 3:
                        pe.wait_ge(*when_empty(("bt", n)))
                        pe.wait_ge(*when_empty(("kt", n)))
                        pe.wait_ge(*turn(("st", n)))
                        b = bank_of(("st", n))
                        for h in range(HEADS):
                            lo, m = 64 * (h % 2), 4 * (h % 2) + h // 2
                            o = b[lo:lo + 64, 64 * (h // 2):64 * (h // 2) + 64]
                            mm(o, b_tok[:, d, 64 * h:64 * h + 64], sa_sb[:, d, 64 * m:64 * m + 64], start=True, stop=False)
                            ins = mm(o, k_tok[:, d, 64 * h:64 * h + 64], vtok[:, c, 64 * h:64 * h + 64], start=False, stop=True)
                        ins.then_inc(*filling(("st", n)))
            pe.wait_ge(S["bonus_in"], 1)
            for j in range(2):
                pe.wait_ge(*turn(("bonus", j)))
                b = bank_of(("bonus", j))
                for i in range(2):
                    ins = mm(b[:, SEQ * i:SEQ * i + SEQ], C("half_ones"), bon[:, 2 * j + i, :], start=True, stop=True)
                ins.then_inc(*filling(("bonus", j)))
            pe.wait_ge(S["y_hat"], 2)
            for j in range(2):
                pe.wait_ge(*turn(("yT", j)))
                b = bank_of(("yT", j))
                for i in range(2):
                    for t in range(2):
                        ins = tr(b[:, (2 * i + t) * P:(2 * i + t + 1) * P], ytok[:, t, P * (2 * j + i):P * (2 * j + i) + P], ident)
                ins.then_inc(*filling(("yT", j)))
            for j in range(2):
                pe.wait_ge(*turn(("gate_b", j)))
                b = bank_of(("gate_b", j))
                for i in range(4):
                    g = small[:, 64 + 4 * j + i:65 + 4 * j + i].to_broadcast([P, P])
                    ins = mm(b[:, P * i:P * i + P], g, ident, start=True, stop=True)
                ins.then_inc(*filling(("gate_b", j)))

            def project_out(l, name, tag):
                for j in range(2):
                    wt = weights((name, j) if l is None else (name, l, j), KD, 512)
                    for t in range(2):
                        pe.wait_ge(*turn((tag, l, j, t)))
                        b = bank_of((tag, l, j, t))
                        for k in range(KD):
                            ins = mm(b[:, :], mixT[:, k, P * t:P * t + P], wt[:, k, :], start=(k == 0), stop=(k == KD - 1))
                        ins.then_inc(*filling((tag, l, j, t)))
                    weights_done((tag, l, j, 1))
            pe.wait_ge(S["mix_rw"], 1)
            for k in range(4):
                pe.wait_ge(*when_empty(("o", k)))
            project_out(None, "out", "out")
            used[0] += 1
            released.append((S["h0"], 2))

            for l in range(DEPTH):
                def to_channels(key, norm):
                    pe.wait_ge(S["xs_a"], 2 * norm + 2)
                    for j in range(4):
                        pe.wait_ge(*turn((key, l, j)))
                        b = bank_of((key, l, j))
                        for i in range(2):
                            for t in range(2):
                                ins = tr(b[:, (2 * i + t) * P:(2 * i + t + 1) * P], xs2[:, t, P * (2 * j + i):P * (2 * j + i) + P], ident)
                        ins.then_inc(*filling((key, l, j)))
                    for j in range(4):
                        pe.wait_ge(*when_empty((key, l, j)))
                to_channels("xa", 2 * l)
                wt = weights(("in2", l, 0), KD, 512)
                for m in range(4):
                    pe.wait_ge(*turn(("u", l, m)))
                    b = bank_of(("u", l, m))
                    for k in range(KD):
                        ins = mm(b[:, 0:SEQ], wt[:, k, P * m:P * m + P], xnT[:, k, :], start=(k == 0), stop=(k == KD - 1))
                    ins.then_inc(*filling(("u", l, m)))
                weights_done(("u", l, 3))
                for n, cols in ((1, 256), (2, 512), (3, 512), (4, 512)):
                    wt = weights(("in2", l, n), KD, cols)
                    for t in range(2):
                        pe.wait_ge(*turn(("tok", l, n, t)))
                        b = bank_of(("tok", l, n, t))
                        for k in range(KD):
                            ins = mm(b[:, 0:cols], xnT[:, k, P * t:P * t + P], wt[:, k, :], start=(k == 0), stop=(k == KD - 1))
                        ins.then_inc(*filling(("tok", l, n, t)))
                    weights_done(("tok", l, n, 1))
                pe.wait_ge(S["p2_load"], 16 * P2_DMAS * (l + 1))
                pe.wait_ge(*turn(("wsT", l)))
                b = bank_of(("wsT", l))
                for h in range(4):
                    ins = tr(b[:, P * h:P * h + P], ws[:, h, :], ident)
                ins.then_inc(*filling(("wsT", l)))
                pe.wait_ge(S["c_masked"], l + 1)
                pe.wait_ge(*turn(("cT", l)))
                b = bank_of(("cT", l))
                for c in range(2):
                    for j in range(2):
                        ins = tr(b[:, (2 * c + j) * P:(2 * c + j + 1) * P], c_rows[:, c, j, :], ident)
                ins.then_inc(*filling(("cT", l)))
                pe.wait_ge(S["b_spread"], l + 1)
                pe.wait_ge(*turn(("bT", l)))
                b = bank_of(("bT", l))
                for j in range(2):
                    for c in range(2):
                        ins = tr(b[:, (2 * j + c) * P:(2 * j + c + 1) * P], bexp[:, j, c].rearrange("p a b -> p (a b)"), ident)
                ins.then_inc(*filling(("bT", l)))
                pe.wait_ge(S["vg_n"], 2 * (l + 1))
                pe.wait_ge(*when_empty(("wsT", l)))
                pe.wait_ge(*turn(("gate", l)))
                b = bank_of(("gate", l))
                for h in range(4):
                    lo = 64 * (h % 2)
                    for t in range(2):
                        ins = mm(b[lo:lo + 64, (2 * (h // 2) + t) * P:(2 * (h // 2) + t + 1) * P], vg[:, t, 64 * h:64 * h + 64], wsT[:, h, :],
                                 start=True, stop=True)
                ins.then_inc(*filling(("gate", l)))
                for c in range(2):
                    pe.wait_ge(S["qk_rot"], 4 * l + 2 * c + 2)
                    for j in range(2):
                        pe.wait_ge(*turn(("qkT", l, c, j)))
                        b = bank_of(("qkT", l, c, j))
                        for i in range(2):
                            for t in range(2):
                                h = 2 * j + i
                                ins = tr(b[:, (2 * i + t) * P:(2 * i + t + 1) * P], qkr[:, c, t, P * h:P * h + P], ident)
                        ins.then_inc(*filling(("qkT", l, c, j)))
                for c in range(2):
                    for j in range(2):
                        pe.wait_ge(*when_empty(("qkT", l, c, j)))
                for t in range(2):
                    pe.wait_ge(*when_empty(("tok", l, 4, t)))
                for i in range(8 + 2):
                    if i < 8:
                        t, h = i // 4, i % 4
                        keys = P * (t + 1)
                        for c in range(2):
                            lo = 64 * c
                            pe.wait_ge(*turn(("ds", l, i, c)))
                            b = bank_of(("ds", l, i, c))
                            mm(b[:, 0:keys], qT2[lo:lo + 64, h, P * t:P * t + P], kT2[lo:lo + 64, h, 0:keys], start=True, stop=False)
                            ins = mm(b[:, keys - P:keys], C("late", 128, 1), C("late", 256, 1)[:, 128:256], start=False, stop=True)
                            ins.then_inc(*filling(("ds", l, i, c)))
                    if 1 <= i <= 8:
                        n = i - 1
                        pe.wait_ge(S["d_w"], 8 * l + n + 1)
                        pe.wait_ge(*turn(("dwT", l, n)))
                        b = bank_of(("dwT", l, n))
                        for k in range(n // 4 + 1):
                            ins = tr(b[:, P * k:P * k + P], prob2[:, n % 2, P * k:P * k + P], ident)
                        ins.then_inc(*filling(("dwT", l, n)))
                    if i >= 2:
                        n = i - 2
                        t, h = n // 4, n % 4
                        pe.wait_ge(*when_empty(("dwT", l, n)))
                        if h == 0:
                            pe.wait_ge(*turn(("do", l, t), "long"))
                            b_o = bank_of(("do", l, t))
                        for k in range(t + 1):
                            ins = mm(b_o[:, P * h:P * h + P], wT2[:, n % 2, P * k:P * k + P], v2[:, k, P * h:P * h + P], start=(k == 0), stop=(k == t))
                        if h == 3:
                            ins.then_inc(*filling(("do", l, t)))
                for m in range(2):
                    pe.wait_ge(*when_empty(("u", l, m)))
                pe.wait_ge(*when_empty(("bT", l)))
                pe.wait_ge(*when_empty(("cT", l)))
                pe.wait_ge(*turn(("ssm_y", l), "long"))
                y = bank_of(("ssm_y", l))
                for s in range(ST + 2):
                    if s < ST:
                        lo, blk = 32 * (s % 4), s // 4
                        pe.wait_ge(*turn(("bu", l, s)))
                        b = bank_of(("bu", l, s))
                        for c in range(2):
                            ins = mm(b[:, SEQ * c:SEQ * c + SEQ], bT[lo:lo + 32, blk, c, :], uT[lo:lo + 32, blk, :], start=True, stop=True)
                        ins.then_inc(*filling(("bu", l, s)))
                    if s >= 2:
                        q = s - 2
                        lo, blk = 32 * (q % 4), q // 4
                        pe.wait_ge(S["rotated"], 2 * (ST * l + q + 1))
                        for f, (ct, pr, half) in enumerate(((0, pr1, 0), (1, pr1, 1), (2, pr2, 0), (2, pr2, 1))):
                            ins = mm(y[lo:lo + 32, SEQ * blk:SEQ * blk + SEQ], cT[:, ct, blk, lo:lo + 32], pr[:, q % 2, SEQ * half:SEQ * half + SEQ],
                                     start=(f == 0), stop=(f == 3))
                        if q < ST - 1:
                            ins.then_inc(S["rotated_used"], 1)
                ins.then_inc(*filling(("ssm_y", l)))
                pe.wait_ge(S["d_hat"], 2 * (l + 1))
                for j in range(2):
                    pe.wait_ge(*turn(("doT", l, j)))
                    b = bank_of(("doT", l, j))
                    for i in range(2):
                        for t in range(2):
                            h = 2 * j + i
                            ins = tr(b[:, (2 * i + t) * P:(2 * i + t + 1) * P], o2[:, t, P * h:P * h + P], ident)
                    ins.then_inc(*filling(("doT", l, j)))
                pe.wait_ge(S["y_gelu"], l + 1)
                pe.wait_ge(*turn(("glu", l)))
                b = bank_of(("glu", l))
                for m in range(2):
                    for k in range(2):
                        ins = mm(b[:, SEQ * m:SEQ * m + SEQ], wglu[:, k, P * m:P * m + P], mixT[:, k, :], start=(k == 0), stop=(k == 1))
                ins.then_inc(*filling(("glu", l)))
                pe.wait_ge(S["mix_ssm"], l + 1)
                pe.wait_ge(S["mix_gmlp"], l + 1)
                for j in range(2):
                    pe.wait_ge(*when_empty(("doT", l, j)))
                project_out(l, "out2", "out2")
                to_channels("xf", 2 * l + 1)
                for n in range(UP_TILES):
                    wt = weights(("up", l, n), 2 * KD, 256)
                    for j in range(PAIRS):
                        m = PAIRS * n + j
                        pe.wait_ge(*turn(("up", l, m)))
                        b = bank_of(("up", l, m))
                        for half in range(2):
                            for k in range(KD):
                                ins = mm(b[:, SEQ * half:SEQ * half + SEQ], wt[:, KD * half + k, P * j:P * j + P], xnT[:, k, :],
                                         start=(k == 0), stop=(k == KD - 1))
                        ins.then_inc(*filling(("up", l, m)))
                    weights_done(("up", l, m))
                pe.wait_ge(*turn(("down", l, 0)))
                pe.wait_ge(*turn(("down", l, 1)))
                pe.wait_ge(*turn(("down", l, 2)))
                pe.wait_ge(*turn(("down", l, 3)))
                acc = [bank_of(("down", l, 0)), bank_of(("down", l, 1)), bank_of(("down", l, 2)), bank_of(("down", l, 3))]
                for n in range(DOWN_TILES):
                    rows = min(DOWN_K, FB - n * DOWN_K)
                    wt = weights(("down", l, n), rows, 1024)
                    for q in range(rows):
                        k = DOWN_K * n + q
                        pe.wait_ge(S["act_T"], FB * l + k + 1)
                        for t in range(2):
                            for j in range(2):
                                ins = mm(acc[2 * t + j][:, :], actT[:, k, P * t:P * t + P], wt[:, q, 512 * j:512 * j + 512],
                                         start=(k == 0), stop=(k == FB - 1))
                                if k == FB - 1:
                                    ins.then_inc(*filling(("down", l, 2 * t + j)))
                    if n < DOWN_TILES - 1:
                        weights_done(ins=ins)
                    else:
                        weights_done(("down", l, 3))

        @block.scalar
        def _(act):
            A = nc.scalar


            act.dma_start(con[:, :], consts).then_inc(S["consts"], 16)
            for j, name in enumerate(("c", "c_ctx")):
                src = w[name].rearrange("a (k p) -> (a k) p", p=P) if name == "c" else w[name].rearrange("(k p) -> k p", p=P)
                act.dma_start(crow[8 * j:8 * j + 8, :], src).then_inc(S["crow"], 16)
            for j, name in enumerate(("x", "ctx")):
                act.dma_start(xc[:, 2 * j:2 * j + 2, :], w[name].rearrange("a (t p) d -> p (a t) d", p=P)).then_inc(S["x_in"], 16)
            rows = {"norm_g": w["norm_g"][0], "mu_prev": w["shift_mu"][0, 0], "mu_next": w["shift_mu"][0, 1], "w0": w["rw_w0"][0].rearrange("d n -> (d n)"),
                    "a0": w["rw_a0"][0].rearrange("d n -> (d n)"), "kk": w["rw_kk"][0], "ka": w["rw_ka"][0], "rk": w["rw_rk"][0].rearrange("h n -> (h n)"),
                    "lnx_g": w["rw_lnx_g"][0], "lnx_b": w["rw_lnx_b"][0], "q_g": w["mla_q_norm_g"][0], "kv_g": w["mla_kv_norm_g"][0],
                    "ada_b": w["ada_b"][0]}
            for name, src in rows.items():
                n = src.shape[0] // P
                act.dma_start(prow[COLS_1[name]:COLS_1[name] + n, :], src.rearrange("(k p) -> k p", p=P)).then_inc(S["params_1"], 16)
            act.dma_start(lev_f, levels).then_inc(S["levels"], 16)
            for j, name in enumerate(("rw_w2", "rw_a2")):
                act.dma_start(lora[:, j, :], w[name][0].rearrange("d e n -> (d e) n")).then_inc(S["lora"], 16)
            for l in range(DEPTH):
                a, b = prow2[:, 2 * l, :], prow2[:, 2 * l + 1, :]
                flat = {"attn_g": "attn_norm_g_2", "ffn_g": "ffn_norm_g_2", "ssm_d": "ssm_d_2", "b_glu": "ssm_b_glu_2", "v_g": "gmlp_v_g_2", "sub_g": "subln_g_2"}
                loads = [(a, COLS_2A["conv01"] + 44 * q, w["conv_w_2"][l, q].rearrange("(k p) -> k p", p=P)) for q in range(2)]
                loads += [(a, COLS_2A[n], w[full_name][l].rearrange("(k p) -> k p", p=P)) for n, full_name in flat.items()]
                loads += [(b, COLS_2B["conv2"], w["conv_w_2"][l, 2].rearrange("(k p) -> k p", p=P)),
                          (b, COLS_2B["conv_b"], w["conv_b_2"][l].rearrange("(k p) -> k p", p=P)),
                          (b, COLS_2B["a_re"], w["ssm_a_re_2"][l].rearrange("(t g) p -> t (g p)", g=2)),
                          (b, COLS_2B["a_im"], w["ssm_a_im_2"][l].rearrange("(t g) p -> t (g p)", g=2))]
                for tile, r, src in loads:
                    act.dma_start(tile[r:r + src.shape[0], :], src).then_inc(S["params_2"], 16)

            act.wait_ge(S["crow"], 32)
            A.activation(cth[0:16, :], crow[0:16, :], ACT.Tanh, scale=0.5).then_inc(S["c_tanh"], 1)
            act.wait_ge(S["x_in"], 32)
            for t in range(4):
                A.activation(junk, xc[:, t, :], ACT.Square, accum_out=small[:, 112 + t:113 + t]).then_inc(S["ssq"], 1)
                act.wait_ge(S["ssq"], t + 1)
            act.wait_ge(S["mod_cols"], 1)
            for k in range(0, KD, 2):
                act.wait_ge(*when_full(("hT", k)))
                b = bank_of(("hT", k))
                for j in range(2):
                    ins = A.activation(hT[:, k, SEQ * j:SEQ * j + SEQ], b[:, SEQ * j:SEQ * j + SEQ], ACT.Identity,
                                       bias=small[:, 32 + 8 * j + k:33 + 8 * j + k], scale=small[:, 16 + 8 * j + k:17 + 8 * j + k])
                ins.then_inc(*emptying(("hT", k)))
            act.wait_ge(S["pads"], 1)
            act.wait_ge(S["c0"], 1)
            shifted = gated = 0
            sq_done = 0
            for blocks in PROJ:
                for kind, i, off, rows_, toks in blocks:
                    key = (kind, i)
                    act.wait_ge(*when_full(key))
                    b = bank_of(key)
                    if kind in MU_BLOCK:
                        m = MU_BLOCK[kind] + i
                        if shifted >= 2:
                            act.wait_ge(S["us"], shifted - 1)
                        segs = toks // SEQ
                        src = b[:, 0:toks].rearrange("p (s n) -> p s n", s=segs)
                        A.activation(ubuf[:, shifted % 2, 0:segs, 1:SEQ + 1], src, ACT.Copy)
                        A.activation(shift_dest(key), b[:, 0:toks], ACT.Identity, scale=small[:, 72 + m:73 + m]).then_inc(*emptying(key))
                        shifted += 1
                        if kind == "w":
                            act.wait_ge(S["us"], US[key])
                            A.activation(usw, usw, ACT.Tanh).then_inc(S["lw_in"], 1)
                    elif kind in ("g", "gm"):
                        if gated >= 2:
                            act.wait_ge(*when_empty(GATES[gated - 2]))
                        A.activation(gtmp[:, gated % 2, :], b[:, 0:SEQ], ACT.Tanh, scale=0.5).then_inc(S["g_tanh"], 1)
                        gated += 1
                    elif kind == "kr":
                        A.activation(krT[0:32, :], b[0:32, :], ACT.Copy).then_inc(*emptying(key))
                    else:
                        lat, sq, g = (lat_q, sq_q, "q_g") if kind == "cq" else (lat_kv, sq_kv, "kv_g")
                        A.activation(lat[:, i, 0:toks], b[:, 0:toks], ACT.Copy, scale=col(g, 1, i))
                        A.activation(sq[:, i, 0:toks], b[:, 0:toks], ACT.Square).then_inc(*emptying(key))
                    if kind == "v":
                        act.wait_ge(S["kkf"], i + 1)
                        A.activation(sqk[:, i, :], kk[:, i, :], ACT.Square).then_inc(S["kk_sq"], 1)
            for t in range(4):
                act.wait_ge(*when_full(("vtok", t)))
                b = bank_of(("vtok", t))
                A.activation(vtok[:, t, :], b[:, :], ACT.Copy).then_inc(*emptying(("vtok", t)))
            act.wait_ge(S["rstd_lat"], 1)
            for t in range(2):
                for j, (a, e) in enumerate(((0, 480), (480, 768))):
                    act.wait_ge(*when_full(("q", t, j)))
                    b = bank_of(("q", t, j))
                    A.activation(qtok[:, t, a:e], b[:, 0:e - a], ACT.Copy, scale=small[:, 126 + t:127 + t]).then_inc(*emptying(("q", t, j)))
            for t in range(4):
                for j in range(2):
                    act.wait_ge(*when_full(("kv", t, j)))
                    b = bank_of(("kv", t, j))
                    src = b[:, :].rearrange("p (h n) -> p h n", h=4)
                    r = small[:, 128 + t:129 + t]
                    A.activation(vm[:, t, SEQ * j:SEQ * j + SEQ].rearrange("p (h n) -> p h n", h=4), src[:, :, 64:128], ACT.Copy, scale=r)
                    A.activation(ktok[:, t, :].rearrange("p (h n) -> p h n", h=8)[:, 4 * j:4 * j + 4, 0:64], src[:, :, 0:64], ACT.Copy, scale=r).then_inc(*emptying(("kv", t, j)))
            for h in range(0, HEADS, 2):
                act.wait_ge(*when_full(("kT", h)))
                b = bank_of(("kT", h))
                A.activation(kT[0:QK, h, :], b[0:QK, :], ACT.Copy).then_inc(*emptying(("kT", h)))
            N = 2 * HEADS
            for i in range(N + 1):
                if i < N:
                    act.wait_ge(*when_full(("s", i)))
                    b = bank_of(("s", i))
                    act.wait_ge(S["m_bias"], i + 1)
                    q = i % 3
                    A.activation(prob[:, q, :], b[:, :], ACT.Exp, bias=small[:, 167 + q:168 + q], scale=ATTN_SCALE,
                                       accum_out=small[:, 170 + q:171 + q]).then_inc(*emptying(("s", i)))
                if i >= 1:
                    act.wait_ge(*when_full(("pT", i - 1)))
                    b = bank_of(("pT", i - 1))
                    A.activation(pT[:, (i - 1) % 2, :], b[:, :], ACT.Copy).then_inc(*emptying(("pT", i - 1)))
            for i in range(4):
                emits = i >= 2
                for d in range(2):
                    n = 2 * i + d
                    if n:
                        act.wait_ge(S["bk_ch"], n)
                    for key, dst, c0 in (("lw", thw, 88), ("la", tha, 96)):
                        act.wait_ge(*when_full((key, n)))
                        b = bank_of((key, n))
                        for k in range(RB):
                            ins = A.activation(dst[:, k, :], b[:, P * k:P * k + P], ACT.Tanh, scale=0.5, bias=small[:, c0 + RB * d + k:c0 + RB * d + k + 1])
                        ins.then_inc(*emptying((key, n)))
                    act.wait_ge(S["decays"], n + 1)
                    A.activation(small[:, 148 + 8 * d:156 + 8 * d], small[:, 132 + 8 * d:140 + 8 * d], ACT.Exp)
                    A.activation(a_ch[:, d], thw if d == 0 else LL, ACT.Exp, scale=1.0 if d == 0 else -1.0)
                    if emits:
                        A.activation(r_ch[:, d], LL if d == 0 else thw, ACT.Exp, scale=1.0 if d == 0 else -1.0)
                    A.activation(E0, LL if d == 0 else thw, ACT.Exp, scale=-1.0 if d == 0 else 1.0).then_inc(S["e_made"], 1)
                    for key, dst in (("bt", b_tok), ("kt", k_tok)):
                        act.wait_ge(*when_full((key, n)))
                        b = bank_of((key, n))
                        A.activation(dst[:, d, :], b[:, :], ACT.Copy).then_inc(*emptying((key, n)))
                for g in range(2):
                    for d in range(2):
                        key = ("t2", 2 * i + d, g)
                        act.wait_ge(*when_full(key))
                        b = bank_of(key)
                        A.activation(TM[:, d].rearrange("p a b -> p (a b)"), b[:, :], ACT.Copy).then_inc(*emptying(key))
                    for e in range(LEVELS):
                        for d in range(2):
                            key = ("x", 2 * i + d, g, e)
                            act.wait_ge(*when_full(key))
                            b = bank_of(key)
                            A.activation(XM[:, d].rearrange("p a b -> p (a b)"), b[:, :], ACT.Copy).then_inc(*emptying(key))
                for d in range(2):
                    for g in range(2):
                        key = ("rhs", 2 * i + d, g)
                        act.wait_ge(*when_full(key))
                        b = bank_of(key)
                        A.activation(rhs_sb[:, d, SEQ * g:SEQ * g + SEQ], b[:, 0:SEQ], ACT.Copy).then_inc(*emptying(key))
            for j in range(2):
                act.wait_ge(*when_full(("yT", j)))
                b = bank_of(("yT", j))
                for i in range(2):
                    k = 2 * j + i
                    ins = A.activation(yn[:, k, :], b[:, SEQ * i:SEQ * i + SEQ], ACT.Identity, scale=col("lnx_g", 1, k), bias=col("lnx_b", 1, k))
                ins.then_inc(*emptying(("yT", j)))
            for j in range(2):
                act.wait_ge(*when_full(("gate_b", j)))
                b = bank_of(("gate_b", j))
                A.activation(gate_b[:, 512 * j:512 * j + 512], b[:, :], ACT.Copy).then_inc(*emptying(("gate_b", j)))
            act.wait_ge(S["x1"], 2)
            for t in range(2):
                A.activation(junk, xc[:, t, :], ACT.Square, accum_out=small[:, 240 + t:241 + t]).then_inc(S["ssq_f"], 1)
                act.wait_ge(S["ssq_f"], t + 1)

            act.wait_ge(S["h0"], 2)
            for l in range(DEPTH):
                def square_sums(norm):
                    for t in range(2):
                        A.activation(junk2, xc[:, t, :], ACT.Square, accum_out=small[:, 256 + t:257 + t]).then_inc(S["ssq_a"], 1)
                        act.wait_ge(S["ssq_a"], 2 * norm + t + 1)

                def channels_even(key, gain):
                    for j in range(0, 4, 2):
                        act.wait_ge(*when_full((key, l, j)))
                        b = bank_of((key, l, j))
                        for i in range(2):
                            k = 2 * j + i
                            ins = A.activation(xnT[:, k, :], b[:, SEQ * i:SEQ * i + SEQ], ACT.Copy, scale=k2(l, gain, 1, k))
                        ins.then_inc(*emptying((key, l, j)))
                if l:
                    act.wait_ge(*when_empty(("down", l - 1, 3)))
                square_sums(2 * l)
                channels_even("xa", "attn_g")
                act.wait_ge(S["p2_load"], 16 * P2_DMAS * (l + 1))
                A.activation(small[:, 384:400], ldt_b, ACT.Exp).then_inc(S["dt_exp"], 1)
                act.wait_ge(S["u_theta"], l + 1)
                A.activation(small[:, 440:448], small[:, 432:440], ACT.Exp)
                A.activation(small[:, 464:480], small[:, 448:464], ACT.Sin, scale=TWO_PI_DOWN).then_inc(S["a_bar_sc"], 1)
                for m in range(2):
                    act.wait_ge(*when_full(("u", l, m)))
                    b = bank_of(("u", l, m))
                    A.activation(uT[:, m, :], b[:, 0:SEQ], ACT.Copy).then_inc(*emptying(("u", l, m)))
                for m in range(2):
                    act.wait_ge(*when_full(("u", l, 2 + m)))
                    b = bank_of(("u", l, 2 + m))
                    A.activation(ug[:, m, :], b[:, 0:SEQ], ACT.Copy).then_inc(*emptying(("u", l, 2 + m)))
                for t in range(2):
                    key = ("tok", l, 1, t)
                    act.wait_ge(*when_full(key))
                    b = bank_of(key)
                    A.activation(vg[:, t, :], b[:, 0:SEQ], ACT.Copy).then_inc(*emptying(key))
                for c in range(2):
                    for t in range(2):
                        key = ("tok", l, 2 + c, t)
                        act.wait_ge(*when_full(key))
                        b = bank_of(key)
                        A.activation(qk[:, c, t, :], b[:, :], ACT.Copy).then_inc(*emptying(key))
                for t in range(2):
                    key = ("tok", l, 4, t)
                    act.wait_ge(*when_full(key))
                    b = bank_of(key)
                    A.activation(v2[:, t, :], b[:, :], ACT.Copy).then_inc(*emptying(key))
                act.wait_ge(S["angle"], 2 * l + 1)
                A.activation(csc[:, :, 1, :], ang, ACT.Sin, scale=TWO_PI_DOWN).then_inc(S["sine"], 1)
                act.wait_ge(S["angle"], 2 * l + 2)
                A.activation(csc[:, :, 0, :], ang, ACT.Sin, scale=TWO_PI_DOWN)
                A.activation(csc[:, :, 2, :], ang, ACT.Sin, scale=TWO_PI_DOWN).then_inc(S["tables"], 1)
                key = ("cT", l)
                act.wait_ge(*when_full(key))
                b = bank_of(key)
                A.activation(cT[:, 0].rearrange("p a b -> p (a b)"), b[:, 0:256], ACT.Copy)
                A.activation(cT[:, 1].rearrange("p a b -> p (a b)"), b[:, 0:256], ACT.Copy, scale=-1.0)
                A.activation(cT[:, 2].rearrange("p a b -> p (a b)"), b[:, 256:512], ACT.Copy, scale=-1.0).then_inc(*emptying(key))
                key = ("bT", l)
                act.wait_ge(*when_full(key))
                b = bank_of(key)
                A.activation(bT.rearrange("p a b c -> p (a b c)"), b[:, :], ACT.Copy).then_inc(*emptying(key))
                for c in range(2):
                    for j in range(2):
                        key = ("qkT", l, c, j)
                        act.wait_ge(*when_full(key))
                        b = bank_of(key)
                        A.activation((qT2, kT2)[c][:, 2 * j:2 * j + 2, :].rearrange("p a b -> p (a b)"), b[:, :], ACT.Copy).then_inc(*emptying(key))
                act.wait_ge(S["lam_sum"], l + 1)
                A.activation(small[:, 362:364], small[:, 360:362], ACT.Exp).then_inc(S["lam_exp"], 1)
                act.wait_ge(S["derived"], l + 1)
                for i in range(8 + 1):
                    if i < 8:
                        keys = P * (i // 4 + 1)
                        act.wait_ge(S["d_bias"], 8 * l + i + 1)
                        for c in range(2):
                            q = 2 * (i % 2) + c
                            act.wait_ge(*when_full(("ds", l, i, c)))
                            b = bank_of(("ds", l, i, c))
                            A.activation(prob2[:, i % 2, SEQ * c:SEQ * c + keys], b[:, 0:keys], ACT.Exp,
                                               bias=small[:, 332 + q:333 + q], scale=0.125, accum_out=small[:, 336 + q:337 + q]).then_inc(*emptying(("ds", l, i, c)))
                    if i >= 1:
                        key = ("dwT", l, i - 1)
                        keys = P * ((i - 1) // 4 + 1)
                        act.wait_ge(*when_full(key))
                        b = bank_of(key)
                        A.activation(wT2[:, (i - 1) % 2, 0:keys], b[:, 0:keys], ACT.Copy).then_inc(*emptying(key))
                for j in range(2):
                    act.wait_ge(*when_full(("doT", l, j)))
                    b = bank_of(("doT", l, j))
                    A.activation(mixT[:, 4 + 2 * j:6 + 2 * j, :].rearrange("p a b -> p (a b)"), b[:, :], ACT.Copy, scale=small[:, 366:367]).then_inc(*emptying(("doT", l, j)))
                act.wait_ge(S["y_cubic"], l + 1)
                A.activation(m2, m2, ACT.Tanh, scale=GELU_C).then_inc(S["y_tanh"], 1)
                act.wait_ge(*when_full(("glu", l)))
                b = bank_of(("glu", l))
                for m in range(2):
                    ins = A.activation(m1[:, SEQ * m:SEQ * m + SEQ], b[:, SEQ * m:SEQ * m + SEQ], ACT.Tanh, scale=0.5, bias=small[:, 368 + m:369 + m])
                ins.then_inc(*emptying(("glu", l)))
                for t in range(2):
                    act.wait_ge(*when_empty(("out2", l, 1, t)))
                square_sums(2 * l + 1)
                channels_even("xf", "ffn_g")
                act.wait_ge(S["hp_pads"], l + 1)

                def gelu_part(m):
                    act.wait_ge(S["gelu_in"], FB * l + m + 1)
                    A.activation(ge[:, m % 2, 1, :], ge[:, m % 2, 0, :], ACT.Tanh, scale=GELU_C).then_inc(S["gelu_tanh"], 1)
                for m in range(FB):
                    act.wait_ge(*when_full(("up", l, m)))
                    b = bank_of(("up", l, m))
                    if m >= 2:
                        act.wait_ge(S["act_T"], FB * l + m - 1)
                    A.activation(hp[:, m % 2, :, 2:SEQ + 2], b[:, :].rearrange("p (a n) -> p a n", a=2), ACT.Copy)
                    for half in range(2):
                        ins = A.activation(cv[:, m % 2, half, :], b[:, SEQ * half:SEQ * half + SEQ], ACT.Identity, scale=k2(l, "conv2", 1, FB * half + m),
                                           bias=k2(l, "conv_b", 1, FB * half + m))
                    ins.then_inc(*emptying(("up", l, m)))
                    if m:
                        gelu_part(m - 1)
                gelu_part(FB - 1)

        @block.vector
        def _(vec):
            V = nc.vector
            TS, TT, STT, TC = V.tensor_scalar, V.tensor_tensor, V.scalar_tensor_tensor, V.tensor_copy



            def per(v, n, count):
                return v.rearrange("p (c o) -> p c o", o=1).to_broadcast([P, count, n])

            def rep(v, count):
                return v.rearrange("p (o n) -> p o n", o=1).to_broadcast([P, count, v.shape[1]])

            vec.wait_ge(S["c_tanh"], 1)
            STT(out=crow[0:16, :], in0=cth[0:16, :], scalar=1.0, in1=crow[0:16, :], op0=ADD, op1=MUL).then_inc(S["c_silu"], 1)
            vec.wait_ge(*when_full("prm"))
            b = bank_of("prm")
            TC(prm[:, 0:COLS_1["all"]], b[:, 0:COLS_1["all"]]).then_inc(*emptying("prm"))
            vec.wait_ge(*when_empty("prm"))
            vec.wait_ge(*when_full("ccol"))
            b = bank_of("ccol")
            TS(small[:, 0:16], b[:, 0:16], 0.5, None, MUL).then_inc(*emptying("ccol"))
            vec.wait_ge(*when_full("prm2"))
            b = bank_of("prm2")
            TC(prm2[:, 0:430], b[:, 0:430]).then_inc(*emptying("prm2"))
            vec.wait_ge(S["ssq"], 4)
            TS(small[:, 116:120], small[:, 112:116], 1.0 / D, EPS, MUL, ADD).then_inc(S["var_1"], 1)
            TT(small[:, 72:86], col("mu_prev", 14), col("mu_next", 14), ADD).then_inc(S["vec_step"], 1)
            vec.wait_ge(S["vec_step"], next(vec_steps))
            TS(small[:, 72:86], small[:, 72:86], -1.0, 1.0, MUL, ADD).then_inc(S["vec_step"], 1)
            vec.wait_ge(S["vec_step"], next(vec_steps))
            TS(small[:, 88:104], col("w0", 16), 0.5, None, MUL).then_inc(S["vec_step"], 1)
            vec.wait_ge(S["vec_step"], next(vec_steps))
            TS(small[:, 104:108], col("ka", 4), 0.5, None, MUL).then_inc(S["vec_step"], 1)
            vec.wait_ge(S["vec_step"], next(vec_steps))
            TS(small[:, 108:112], col("ka", 4), -0.5, 1.0, MUL, ADD).then_inc(S["c0"], 1)
            vec.wait_ge(S["rstd_1"], 1)
            for t in range(4):
                TS(xs[:, t, :], xc[:, t, :], small[:, 116 + t:117 + t], None, MUL).then_inc(S["xs"], 1)
            vec.wait_ge(*when_full("mod"))
            b = bank_of("mod")[:, 0:48].rearrange("p (m j) -> p j m", j=2)
            for j in range(2):
                TT(small[:, 32 + 8 * j:40 + 8 * j], b[:, j, 0:8], col("ada_b", 8), ADD).then_inc(S["vec_step"], 1)
                vec.wait_ge(S["vec_step"], next(vec_steps))
                TT(small[:, 16 + 8 * j:24 + 8 * j], b[:, j, 8:16], col("ada_b", 8, 8), ADD).then_inc(S["vec_step"], 1)
                vec.wait_ge(S["vec_step"], next(vec_steps))
            TT(small[:, 64:72], b[:, 0, 16:24], col("ada_b", 8, 16), ADD).then_inc(*emptying("mod"))
            vec.wait_ge(*when_empty("mod"))
            STT(out=small[:, 16:24], in0=small[:, 16:24], scalar=1.0, in1=col("norm_g", 8), op0=ADD, op1=MUL).then_inc(S["vec_step"], 1)
            vec.wait_ge(S["vec_step"], next(vec_steps))
            ins = STT(out=small[:, 24:32], in0=small[:, 24:32], scalar=1.0, in1=col("norm_g", 8), op0=ADD, op1=MUL)
            ins.then_inc(S["mod_cols"], 1)
            vec.wait_ge(S["mod_cols"], 1)
            for k in range(1, KD, 2):
                vec.wait_ge(*when_full(("hT", k)))
                b = bank_of(("hT", k))
                for j in range(2):
                    ins = TS(hT[:, k, SEQ * j:SEQ * j + SEQ], b[:, SEQ * j:SEQ * j + SEQ], small[:, 16 + 8 * j + k:17 + 8 * j + k],
                             small[:, 32 + 8 * j + k:33 + 8 * j + k], MUL, ADD)
                ins.then_inc(*emptying(("hT", k)))
            shifted = gated = 0
            for blocks in PROJ:
                for kind, i, off, rows_, toks in blocks:
                    key = (kind, i)
                    if kind in MU_BLOCK:
                        m, segs = MU_BLOCK[kind] + i, toks // SEQ
                        vec.wait_ge(*when_empty(key))
                        dst = shift_dest(key)[:, 0:toks].rearrange("p (s n) -> p s n", s=segs)
                        u = ubuf[:, shifted % 2, 0:segs, :]
                        STT(out=dst, in0=u[:, :, 0:SEQ], scalar=col("mu_prev", 1, m), in1=dst, op0=MUL, op1=ADD).then_inc(S["vec_step"], 1)
                        vec.wait_ge(S["vec_step"], next(vec_steps))
                        STT(out=dst, in0=u[:, :, 2:SEQ + 2], scalar=col("mu_next", 1, m), in1=dst, op0=MUL, op1=ADD).then_inc(S["us"], 1)
                        shifted += 1
                        if kind == "k":
                            vec.wait_ge(S["us"], US[key])
                            TS(kk[:, i, :], kb[:, i, :], col("kk", 1, i), None, MUL).then_inc(S["kkf"], 1)
                    elif kind in ("g", "gm"):
                        vec.wait_ge(*when_full(key))
                        b = bank_of(key)
                        gated += 1
                        vec.wait_ge(S["g_tanh"], gated)
                        STT(out=(grw if kind == "g" else gm)[:, i, :], in0=gtmp[:, (gated - 1) % 2, :], scalar=1.0, in1=b[:, 0:SEQ], op0=ADD, op1=MUL).then_inc(*emptying(key))
            vec.wait_ge(*when_full("lat_ssq"))
            b = bank_of("lat_ssq")
            TS(small[:, 120:122], b[:, 0:2], 1.0 / Q_LORA, EPS, MUL, ADD).then_inc(S["vec_step"], 1)
            vec.wait_ge(S["vec_step"], next(vec_steps))
            TS(small[:, 122:126], b[:, 2:6], 1.0 / KV_LORA, EPS, MUL, ADD).then_inc(*emptying("lat_ssq"))

            def rotate(v, t):
                n = v.shape[1]
                v = v.rearrange("p h (a f n) -> p h a f n", a=2, f=2)
                cs, sn = (C(name, 32)[:, 16 * t:16 * t + 16].rearrange("p (o a n) -> p o a n", o=1, a=2).to_broadcast([P, n, 2, 8]) for name in ("cos_ax", "sin_ax"))
                r = [rtmp[:, q, 0:16 * n].rearrange("p (h a n) -> p h a n", h=n, a=2) for q in range(4)]
                TT(r[0], v[:, :, :, 0, :], cs, MUL).then_inc(S["vec_step"], 1)
                vec.wait_ge(S["vec_step"], next(vec_steps))
                TT(r[1], v[:, :, :, 1, :], sn, MUL).then_inc(S["vec_step"], 1)
                vec.wait_ge(S["vec_step"], next(vec_steps))
                TT(r[2], v[:, :, :, 0, :], sn, MUL).then_inc(S["vec_step"], 1)
                vec.wait_ge(S["vec_step"], next(vec_steps))
                TT(r[3], v[:, :, :, 1, :], cs, MUL).then_inc(S["vec_step"], 1)
                vec.wait_ge(S["vec_step"], next(vec_steps))
                TT(v[:, :, :, 0, :], r[0], r[1], SUB).then_inc(S["vec_step"], 1)
                vec.wait_ge(S["vec_step"], next(vec_steps))
                return TT(v[:, :, :, 1, :], r[2], r[3], ADD)
            vec.wait_ge(*when_full("krt"))
            b = bank_of("krt")
            TC(krt, b[:, 0:128].rearrange("p (t n) -> p t n", t=4)).then_inc(*emptying("krt"))
            vec.wait_ge(*when_empty("krt"))
            for t in range(2):
                rotate(krt[:, t:t + 1, :], t).then_inc(S["vec_step"], 1)
                vec.wait_ge(S["vec_step"], next(vec_steps))
            vec.wait_ge(*when_full("kk_len"))
            b = bank_of("kk_len")
            TS(rn[0:8, :], b[0:8, :], 1e-24, None, MAX).then_inc(*emptying("kk_len"))
            for t in range(4):
                TC(ktok[:, t, :].rearrange("p (h n) -> p h n", h=8)[:, :, 64:96], krt[:, t:t + 1, :].to_broadcast([P, 8, 32])).then_inc(S["k_tok"], 1)
            for t in range(2):
                vec.wait_ge(*when_empty(("q", t, 1)))
                rotate(qtok[:, t, :].rearrange("p (h n) -> p h n", h=8)[:, :, 64:96], t).then_inc(S["q_tok"], 1)
                vec.wait_ge(S["q_tok"], t + 1)
            for k in range(RB):
                vec.wait_ge(*when_full(("kk_x", k)))
                b = bank_of(("kk_x", k))
                TT(kk[:, k, :], kk[:, k, :], b[:, :], MUL).then_inc(*emptying(("kk_x", k)))
            for j in range(4):
                vec.wait_ge(*when_full(("qT", j)))
                b = bank_of(("qT", j))
                TC(qT[0:QK, 2 * j:2 * j + 2, :].rearrange("p a b -> p (a b)"), b[0:QK, :]).then_inc(*emptying(("qT", j)))
            for h in range(1, HEADS, 2):
                vec.wait_ge(*when_full(("kT", h)))
                b = bank_of(("kT", h))
                TC(kT[0:QK, h, :], b[0:QK, :]).then_inc(*emptying(("kT", h)))
            N = 2 * HEADS

            def take_o(k):
                vec.wait_ge(*when_full(("o", k)))
                b = bank_of(("o", k))
                STT(out=mixT[:, 4 + k, :], in0=b[:, 0:SEQ], scalar=0.5, in1=gm[:, k, :], op0=MUL, op1=MUL).then_inc(*emptying(("o", k)))
            for i in range(N + 1):
                if i < N:
                    q = i % 3
                    vec.wait_ge(*when_full(("s", i)))
                    b = bank_of(("s", i))
                    V.tensor_reduce(small[:, 164 + q:165 + q], b[:, :], AX_X, MAX, negate=True).then_inc(S["vec_step"], 1)
                    vec.wait_ge(S["vec_step"], next(vec_steps))
                    TS(small[:, 167 + q:168 + q], small[:, 164 + q:165 + q], ATTN_SCALE, None, MUL).then_inc(S["m_bias"], 1)
                if i >= 1:
                    q = (i - 1) % 3
                    vec.wait_ge(*when_empty(("s", i - 1)))
                    V.reciprocal(small[:, 173 + q:174 + q], small[:, 170 + q:171 + q]).then_inc(S["vec_step"], 1)
                    vec.wait_ge(S["vec_step"], next(vec_steps))
                    TS(prob[:, q, :], prob[:, q, :], small[:, 173 + q:174 + q], None, MUL).then_inc(S["m_prob"], 1)
                if i >= 6 and (i - 6) % 4 == 0:
                    take_o((i - 6) // 4)
            take_o(3)
            vec.wait_ge(S["levels"], 17)

            def gram(dst, key, mask):
                vec.wait_ge(*when_full(key))
                b = bank_of(key)
                TT(dst, b[:, :].rearrange("p (a b) -> p a b", a=4), rep(C(mask), 4), MUL).then_inc(*emptying(key))
            for i in range(4):
                emits = i >= 2
                for d in range(2):
                    n, c = 2 * i + d, ORDER[d][i]
                    tok = slice(P * c, P * c + P)
                    vec.wait_ge(*when_empty(("la", n)))
                    TS(thw, thw, -0.5 * DECAY, -0.5 * DECAY, MUL, ADD).then_inc(S["vec_step"], 1)
                    vec.wait_ge(S["vec_step"], next(vec_steps))
                    for k in range(RB):
                        ins = V.tensor_tensor_scan(LL[:, k, :], C("ones"), thw[:, k, :], 0.0, MUL, ADD)
                    ins.then_inc(S["vec_step"], 1)
                    vec.wait_ge(S["vec_step"], next(vec_steps))
                    dec = small[:, 132 + 8 * d:140 + 8 * d]
                    TC(dec[:, 0:4], LL[:, :, 63]).then_inc(S["vec_step"], 1)
                    vec.wait_ge(S["vec_step"], next(vec_steps))
                    TT(dec[:, 4:8], LL[:, :, 127], dec[:, 0:4], SUB).then_inc(S["vec_step"], 1)
                    vec.wait_ge(S["vec_step"], next(vec_steps))
                    TT(LL, LL, per(dec[:, 0:4], P, 4), SUB).then_inc(S["vec_step"], 1)
                    vec.wait_ge(S["vec_step"], next(vec_steps))
                    TT(thw, LL, thw, SUB).then_inc(S["decays"], 1)
                    if n:
                        vec.wait_ge(*when_full(("rk" if (n - 1) // 2 >= 2 else "ak", n - 1, 1)))
                    for k in range(RB):
                        TS(k_ch[:, k, :], tha[:, k, :], small[:, 104 + k:105 + k], small[:, 108 + k:109 + k], MUL, ADD).then_inc(S["vec_step"], 1)
                        vec.wait_ge(S["vec_step"], next(vec_steps))
                    STT(out=b_ch, in0=tha, scalar=1.0, in1=kk[:, :, tok], op0=ADD, op1=MUL).then_inc(S["vec_step"], 1)
                    vec.wait_ge(S["vec_step"], next(vec_steps))
                    TT(k_ch, k_ch, kb[:, :, tok], MUL).then_inc(S["vec_step"], 1)
                    vec.wait_ge(S["vec_step"], next(vec_steps))
                    vec.wait_ge(S["e_made"], n + 1)
                    STT(out=a_ch[:, d], in0=a_ch[:, d], scalar=-1.0, in1=kk[:, :, tok], op0=MUL, op1=MUL).then_inc(S["vec_step"], 1)
                    vec.wait_ge(S["vec_step"], next(vec_steps))
                    if emits:
                        TT(r_ch[:, d], r_ch[:, d], rb[:, :, tok], MUL).then_inc(S["vec_step"], 1)
                        vec.wait_ge(S["vec_step"], next(vec_steps))
                        if i == 2:
                            TC(kds[:, :, tok], k_ch).then_inc(S["vec_step"], 1)
                            vec.wait_ge(S["vec_step"], next(vec_steps))
                        else:
                            TT(kds[:, :, tok], kds[:, :, tok], k_ch, ADD).then_inc(S["vec_step"], 1)
                            vec.wait_ge(S["vec_step"], next(vec_steps))
                    if i:
                        inward = small[:, 148 + 8 * d + 4 * d:152 + 8 * d + 4 * d]
                        TT(state[:, d], state[:, d], per(inward, 64, 4), MUL).then_inc(S["s_in"], 1)
                    TT(k_ch, k_ch, E0, MUL).then_inc(S["vec_step"], 1)
                    vec.wait_ge(S["vec_step"], next(vec_steps))
                    STT(out=b_ch, in0=b_ch, scalar=0.5, in1=E0, op0=MUL, op1=MUL).then_inc(S["bk_ch"], 1)
                    side = "up" if d == 0 else "lo"
                    for g in range(2):
                        gram(NT[:, d, g], ("nt", n, g), side + "_strict")
                        gram(AK[:, d, 4 * g:4 * g + 4], ("ak", n, g), side + "_strict")
                        if emits:
                            gram(RBm[:, d, 4 * g:4 * g + 4], ("rb", n, g), side + "_incl")
                            gram(RKm[:, d, 4 * g:4 * g + 4], ("rk", n, g), side + "_incl")
                    vec.wait_ge(*when_empty(("nt", n, 1)))
                for g in range(2):
                    for d in range(2):
                        q = QM[:, d, 4 * g:4 * g + 4]
                        TT(q, NT[:, d, g], rep(C("up_1" if d == 0 else "lo_1"), 4), MUL).then_inc(S["vec_step"], 1)
                        vec.wait_ge(S["vec_step"], next(vec_steps))
                        TT(q, q, rep(C("ident"), 4), ADD).then_inc(S["q2"], 1)
                for g in range(2):
                    for e in range(LEVELS):
                        for d in range(2):
                            n = 2 * i + d
                            lower, upper = (rep(lev[:, P * (e + o):P * (e + o) + P], 4) for o in (0, LEVELS))
                            if e < LEVELS - 1:
                                key = ("p", n, g, e)
                                vec.wait_ge(*when_full(key))
                                b = bank_of(key)
                                V.copy_predicated(TM[:, d], lower if d == 0 else upper, b[:, :].rearrange("p (a b) -> p a b", a=4)).then_inc(*emptying(key))
                            key = ("pq", n, g, e)
                            vec.wait_ge(*when_full(key))
                            b = bank_of(key)
                            V.copy_predicated(QM[:, d, 4 * g:4 * g + 4], upper if d == 0 else lower, b[:, :].rearrange("p (a b) -> p a b", a=4)).then_inc(*emptying(key))
                for d in range(2):
                    key = ("sa", 2 * i + d)
                    vec.wait_ge(*when_full(key))
                    b = bank_of(key)
                    TC(sa_sb[:, d, :], b[:, :]).then_inc(*emptying(key))
                for d in range(2):
                    n, c = 2 * i + d, ORDER[d][i]
                    if emits:
                        for g in range(2):
                            vec.wait_ge(*when_full(("y", n, g)))
                            b = bank_of(("y", n, g))[:, 0:SEQ].rearrange("p (j n) -> p j n", j=4)
                            o = ytok[:, c, :].rearrange("p (j g n) -> p g j n", g=2, n=64)[:, g]
                            (TC(o, b) if i == 2 else TT(o, o, b, ADD)).then_inc(*emptying(("y", n, g)))
                            vec.wait_ge(*when_empty(("y", n, g)))
                    if i < 3:
                        vec.wait_ge(*when_full(("st", n)))
                        b = bank_of(("st", n))[:, 0:256].rearrange("p (b n) -> p b n", b=4)
                        outward = small[:, 152 + 8 * d - 4 * d:156 + 8 * d - 4 * d]
                        if i:
                            TT(state[:, d], state[:, d], b, ADD).then_inc(*emptying(("st", n)))
                            vec.wait_ge(*when_empty(("st", n)))
                            TT(state[:, d], state[:, d], per(outward, 64, 4), MUL).then_inc(S["vec_step"], 1)
                            vec.wait_ge(S["vec_step"], next(vec_steps))
                        else:
                            TT(state[:, d], b, per(outward, 64, 4), MUL).then_inc(*emptying(("st", n)))
                            vec.wait_ge(*when_empty(("st", n)))
            for k in range(RB):
                ins = STT(out=bon[:, k, :], in0=kds[:, k, :], scalar=col("rk", 1, k), in1=rb[:, k, :], op0=MUL, op1=MUL)
            ins.then_inc(S["bonus_in"], 1)
            for t in range(2):
                y3 = ytok[:, t, :].rearrange("p (h n) -> p h n", h=8)
                q3 = ysq[:, t, :].rearrange("p (h n) -> p h n", h=8)
                mean, var = small[:, 192 + 8 * t:200 + 8 * t], small[:, 208 + 8 * t:216 + 8 * t]
                V.tensor_reduce(mean, y3, AX_X, ADD).then_inc(S["vec_step"], 1)
                vec.wait_ge(S["vec_step"], next(vec_steps))
                TS(mean, mean, 1.0 / HEAD, None, MUL).then_inc(S["vec_step"], 1)
                vec.wait_ge(S["vec_step"], next(vec_steps))
                TT(y3, y3, per(mean, 64, 8), SUB).then_inc(S["vec_step"], 1)
                vec.wait_ge(S["vec_step"], next(vec_steps))
                TT(q3, y3, y3, MUL).then_inc(S["vec_step"], 1)
                vec.wait_ge(S["vec_step"], next(vec_steps))
                V.tensor_reduce(var, q3, AX_X, ADD).then_inc(S["vec_step"], 1)
                vec.wait_ge(S["vec_step"], next(vec_steps))
                TS(var, var, 1.0 / HEAD, LNX_EPS, MUL, ADD).then_inc(S["y_var"], 1)
            for j in range(2):
                vec.wait_ge(*when_full(("bonus", j)))
                b = bank_of(("bonus", j))
                TT(bon[:, 2 * j:2 * j + 2, :], b[:, :].rearrange("p (a n) -> p a n", a=2), vb[:, 2 * j:2 * j + 2, 0:SEQ], MUL).then_inc(*emptying(("bonus", j)))
            vec.wait_ge(S["y_rstd"], 2)
            for t in range(2):
                y3 = ytok[:, t, :].rearrange("p (h n) -> p h n", h=8)
                TT(y3, y3, per(small[:, 208 + 8 * t:216 + 8 * t], 64, 8), MUL).then_inc(S["y_hat"], 1)
            for j in range(2):
                vec.wait_ge(*when_empty(("yT", j)))
            for j in range(2):
                vec.wait_ge(*when_empty(("bonus", j)))
            TT(bon, bon, yn, ADD).then_inc(S["vec_step"], 1)
            vec.wait_ge(S["vec_step"], next(vec_steps))
            STT(out=mixT[:, 0:4, :].rearrange("p a b -> p (a b)"), in0=bon.rearrange("p a b -> p (a b)"), scalar=0.5, in1=grw.rearrange("p a b -> p (a b)"), op0=MUL, op1=MUL).then_inc(S["mix_rw"], 1)
            for j in range(2):
                vec.wait_ge(*when_empty(("gate_b", j)))
                for t in range(2):
                    vec.wait_ge(*when_full(("out", None, j, t)))
                    b = bank_of(("out", None, j, t))
                    cols = slice(512 * j, 512 * j + 512)
                    TT(xtmp, b[:, :], gate_b[:, cols], MUL).then_inc(*emptying(("out", None, j, t)))
                    vec.wait_ge(*when_empty(("out", None, j, t)))
                    ins = TT(xc[:, t, cols], xc[:, t, cols], xtmp, ADD)
                    if j:
                        ins.then_inc(S["x1"], 1)
                        vec.wait_ge(S["x1"], t + 1)
                    else:
                        ins.then_inc(S["vec_step"], 1)
                        vec.wait_ge(S["vec_step"], next(vec_steps))
            vec.wait_ge(S["ssq_f"], 2)
            TS(small[:, 240:242], small[:, 240:242], 1.0 / D, EPS, MUL, ADD).then_inc(S["var_f"], 1)
            vec.wait_ge(S["rstd_f"], 1)
            n = index["final_g"]
            vec.wait_ge(slot_full[slot_of[n]], 32 * fills[n])
            for t in range(2):
                STT(out=xc[:, t, :], in0=xc[:, t, :], scalar=small[:, 242 + t:243 + t], in1=slot(n)[:, 0:D], op0=MUL, op1=MUL).then_inc(S["h0"], 1)
            vec.wait_ge(S["h0"], 2)

            for l in range(DEPTH):
                def norm(n):
                    vec.wait_ge(S["ssq_a"], 2 * n + 2)
                    TS(small[:, 256:258], small[:, 256:258], 1.0 / D, EPS, MUL, ADD).then_inc(S["var_a"], 1)
                    vec.wait_ge(S["rstd_a"], n + 1)
                    for t in range(2):
                        TS(xs2[:, t, :], xc[:, t, :], small[:, 258 + t:259 + t], None, MUL).then_inc(S["xs_a"], 1)

                def channels_odd(key, gain):
                    for j in range(1, 4, 2):
                        vec.wait_ge(*when_full((key, l, j)))
                        b = bank_of((key, l, j))
                        for i in range(2):
                            k = 2 * j + i
                            ins = TS(xnT[:, k, :], b[:, SEQ * i:SEQ * i + SEQ], k2(l, gain, 1, k), None, MUL)
                        ins.then_inc(*emptying((key, l, j)))
                norm(2 * l)
                channels_odd("xa", "attn_g")
                vec.wait_ge(S["p2_load"], 16 * P2_DMAS * (l + 1))
                vec.wait_ge(S["dt_exp"], l + 1)
                are, aim = k2(l, "a_re", 8), k2(l, "a_im", 8)

                def sc(a, n=8):
                    return small[:, a:a + n]
                par = C("state_par", 2)
                dts = small[:, 384:400].rearrange("p (t g) -> p g t", g=2)
                TS(sc(400), dts[:, 0], par[:, 0:1], None, MUL).then_inc(S["vec_step"], 1)
                vec.wait_ge(S["vec_step"], next(vec_steps))
                STT(out=sc(400), in0=dts[:, 1], scalar=par[:, 1:2], in1=sc(400), op0=MUL, op1=ADD).then_inc(S["vec_step"], 1)
                vec.wait_ge(S["vec_step"], next(vec_steps))
                TT(sc(432), are, sc(400), MUL).then_inc(S["vec_step"], 1)
                vec.wait_ge(S["vec_step"], next(vec_steps))
                TT(sc(408), aim, sc(400), MUL).then_inc(S["vec_step"], 1)
                vec.wait_ge(S["vec_step"], next(vec_steps))
                TS(sc(416), sc(408), 1.0 / TWO_PI, None, MUL).then_inc(S["vec_step"], 1)
                vec.wait_ge(S["vec_step"], next(vec_steps))
                TS(sc(416), sc(416), ROUND, None, ADD).then_inc(S["vec_step"], 1)
                vec.wait_ge(S["vec_step"], next(vec_steps))
                TS(sc(416), sc(416), -ROUND, None, ADD).then_inc(S["vec_step"], 1)
                vec.wait_ge(S["vec_step"], next(vec_steps))
                for part in PI_PARTS:
                    STT(out=sc(408), in0=sc(416), scalar=-part, in1=sc(408), op0=MUL, op1=ADD).then_inc(S["vec_step"], 1)
                    vec.wait_ge(S["vec_step"], next(vec_steps))
                TS(sc(448), sc(408), 1.0 / TWO_PI, None, MUL).then_inc(S["vec_step"], 1)
                vec.wait_ge(S["vec_step"], next(vec_steps))
                TS(sc(456), sc(448), 0.25, None, ADD).then_inc(S["vec_step"], 1)
                vec.wait_ge(S["vec_step"], next(vec_steps))
                TS(sc(416), sc(456), ROUND, None, ADD).then_inc(S["vec_step"], 1)
                vec.wait_ge(S["vec_step"], next(vec_steps))
                TS(sc(416), sc(416), -ROUND, None, ADD).then_inc(S["vec_step"], 1)
                vec.wait_ge(S["vec_step"], next(vec_steps))
                TT(sc(456), sc(456), sc(416), SUB).then_inc(S["u_theta"], 1)
                vec.wait_ge(S["a_bar_sc"], l + 1)
                TT(sc(488), sc(440), sc(472), MUL).then_inc(S["vec_step"], 1)
                vec.wait_ge(S["vec_step"], next(vec_steps))
                TT(sc(496), sc(440), sc(464), MUL).then_inc(S["vec_step"], 1)
                vec.wait_ge(S["vec_step"], next(vec_steps))
                TS(sc(488), sc(488), -1.0, None, ADD).then_inc(S["vec_step"], 1)
                vec.wait_ge(S["vec_step"], next(vec_steps))
                TT(sc(416), are, are, MUL).then_inc(S["vec_step"], 1)
                vec.wait_ge(S["vec_step"], next(vec_steps))
                TT(sc(424), aim, aim, MUL).then_inc(S["vec_step"], 1)
                vec.wait_ge(S["vec_step"], next(vec_steps))
                TT(sc(424), sc(424), sc(416), ADD).then_inc(S["vec_step"], 1)
                vec.wait_ge(S["vec_step"], next(vec_steps))
                V.reciprocal(sc(424), sc(424)).then_inc(S["vec_step"], 1)
                vec.wait_ge(S["vec_step"], next(vec_steps))
                TT(sc(400), sc(488), are, MUL).then_inc(S["vec_step"], 1)
                vec.wait_ge(S["vec_step"], next(vec_steps))
                TT(sc(416), sc(496), aim, MUL).then_inc(S["vec_step"], 1)
                vec.wait_ge(S["vec_step"], next(vec_steps))
                TT(sc(400), sc(400), sc(416), ADD).then_inc(S["vec_step"], 1)
                vec.wait_ge(S["vec_step"], next(vec_steps))
                TT(sc(504), sc(496), are, MUL).then_inc(S["vec_step"], 1)
                vec.wait_ge(S["vec_step"], next(vec_steps))
                TT(sc(416), sc(488), aim, MUL).then_inc(S["vec_step"], 1)
                vec.wait_ge(S["vec_step"], next(vec_steps))
                TT(sc(504), sc(504), sc(416), SUB).then_inc(S["vec_step"], 1)
                vec.wait_ge(S["vec_step"], next(vec_steps))
                TT(sc(400), sc(400), sc(424), MUL).then_inc(S["vec_step"], 1)
                vec.wait_ge(S["vec_step"], next(vec_steps))
                TT(sc(504), sc(504), sc(424), MUL).then_inc(S["vec_step"], 1)
                vec.wait_ge(S["vec_step"], next(vec_steps))
                TT(tb[:, 0], per(sc(400), 16, 8), b_rows[:, 0], MUL).then_inc(S["vec_step"], 1)
                vec.wait_ge(S["vec_step"], next(vec_steps))
                TT(tb[:, 1], per(sc(504), 16, 8), b_rows[:, 1], MUL).then_inc(S["vec_step"], 1)
                vec.wait_ge(S["vec_step"], next(vec_steps))
                TT(tb[:, 2], per(sc(400), 16, 8), b_rows[:, 1], MUL).then_inc(S["vec_step"], 1)
                vec.wait_ge(S["vec_step"], next(vec_steps))
                TT(tb[:, 3], per(sc(504), 16, 8), b_rows[:, 0], MUL).then_inc(S["vec_step"], 1)
                vec.wait_ge(S["vec_step"], next(vec_steps))
                TT(tb[:, 0], tb[:, 0], tb[:, 1], SUB).then_inc(S["vec_step"], 1)
                vec.wait_ge(S["vec_step"], next(vec_steps))
                TT(tb[:, 2], tb[:, 2], tb[:, 3], ADD).then_inc(S["vec_step"], 1)
                vec.wait_ge(S["vec_step"], next(vec_steps))
                for c in range(2):
                    for g in range(2):
                        for j in range(2):
                            ins = TS(bexp[:, j, c, :, 16 * g:16 * g + 16], tb[:, 2 * c, 4 * j:4 * j + 4, :], par[:, g:g + 1], None, MUL)
                ins.then_inc(S["b_spread"], 1)
                crs = c_rows.rearrange("p a b c -> p (a b) c")
                TT(crs, crs, rep(C("group_par"), 4), MUL).then_inc(S["c_masked"], 1)
                vec.wait_ge(*when_full(("wsT", l)))
                b = bank_of(("wsT", l))
                TT(wsT, b[:, :].rearrange("p (a b) -> p a b", a=4), rep(C("window"), 4), MUL).then_inc(*emptying(("wsT", l)))
                vec.wait_ge(S["angle_raw"], l + 1)
                k_turns = csc[:, :, 2, :]
                TS(k_turns, ang, ROUND, None, ADD).then_inc(S["vec_step"], 1)
                vec.wait_ge(S["vec_step"], next(vec_steps))
                TS(k_turns, k_turns, -ROUND, None, ADD).then_inc(S["vec_step"], 1)
                vec.wait_ge(S["vec_step"], next(vec_steps))
                TT(ang, ang, k_turns, SUB).then_inc(S["angle"], 1)
                vec.wait_ge(S["sine"], l + 1)
                TS(ang, ang, 0.25, None, ADD).then_inc(S["vec_step"], 1)
                vec.wait_ge(S["vec_step"], next(vec_steps))
                TS(k_turns, ang, ROUND, None, ADD).then_inc(S["vec_step"], 1)
                vec.wait_ge(S["vec_step"], next(vec_steps))
                TS(k_turns, k_turns, -ROUND, None, ADD).then_inc(S["vec_step"], 1)
                vec.wait_ge(S["vec_step"], next(vec_steps))
                TT(ang, ang, k_turns, SUB).then_inc(S["angle"], 1)
                for c in range(2):
                    for t in range(2):
                        cs, sn = (rep(C(name, 64)[:, 32 * t:32 * t + 32], 2) for name in ("cos_d", "sin_d"))
                        TT(tabs[:, c, 0, t, :].rearrange("p (f n) -> p f n", f=2), gains[:, 2 * c, :].rearrange("p (f n) -> p f n", f=2), cs, MUL).then_inc(S["vec_step"], 1)
                        vec.wait_ge(S["vec_step"], next(vec_steps))
                        ins = TT(tabs[:, c, 1, t, :].rearrange("p (f n) -> p f n", f=2), gains[:, 2 * c + 1, :].rearrange("p (f n) -> p f n", f=2), sn, MUL)
                ins.then_inc(S["vec_step"], 1)
                vec.wait_ge(S["vec_step"], next(vec_steps))
                for c in range(2):
                    ins = TS(tabs[:, c, 1, :, 0:32], tabs[:, c, 1, :, 0:32], -1.0, None, MUL)
                ins.then_inc(S["vec_step"], 1)
                vec.wait_ge(S["vec_step"], next(vec_steps))
                lam_init = 0.8 - 0.6 * math.exp(-0.3 * l)
                TT(lam_b[:, 0:2, :], lam_b[:, 0:2, :], lam_b[:, 2:4, :], MUL).then_inc(S["vec_step"], 1)
                vec.wait_ge(S["vec_step"], next(vec_steps))
                V.tensor_reduce(small[:, 360:362], lam_b[:, 0:2, :], AX_X, ADD).then_inc(S["lam_sum"], 1)
                TS(small[:, 366:367], k2(l, "sub_g"), 1.0 - lam_init, None, MUL).then_inc(S["vec_step"], 1)
                vec.wait_ge(S["vec_step"], next(vec_steps))
                TS(small[:, 368:370], k2(l, "b_glu", 2), 0.5, None, MUL).then_inc(S["derived"], 1)
                vec.wait_ge(*when_empty(("tok", l, 1, 1)))
                for t in range(2):
                    STT(out=vtmp[:, 0:SEQ], in0=vg[:, t, :], scalar=1.0, in1=vg[:, t, :], op0=MUL, op1=MUL, accum_out=small[:, 260 + t:261 + t]).then_inc(S["vec_step"], 1)
                    vec.wait_ge(S["vec_step"], next(vec_steps))
                TS(small[:, 260:262], small[:, 260:262], 1.0 / SEQ, EPS, MUL, ADD).then_inc(S["vg_var"], 1)
                vec.wait_ge(S["vg_rstd"], l + 1)
                for t in range(2):
                    TS(vg[:, t, :], vg[:, t, :], small[:, 262 + t:263 + t], None, MUL).then_inc(S["vg_n"], 1)
                for c in range(2):
                    vec.wait_ge(*when_empty(("tok", l, 2 + c, 1)))
                    for t in range(2):
                        TT(vtmp, qk[:, c, t, :], qk[:, c, t, :], MUL).then_inc(S["vec_step"], 1)
                        vec.wait_ge(S["vec_step"], next(vec_steps))
                        a = 264 + 16 * c + 8 * t
                        V.tensor_reduce(small[:, a:a + 8], vtmp.rearrange("p (h n) -> p h n", h=8), AX_X, ADD).then_inc(S["vec_step"], 1)
                        vec.wait_ge(S["vec_step"], next(vec_steps))
                TS(small[:, 264:296], small[:, 264:296], 1.0 / 64, EPS, MUL, ADD).then_inc(S["qk_var"], 1)
                vec.wait_ge(S["qk_rstd"], l + 1)
                vec.wait_ge(S["tables"], l + 1)
                for c in range(2):
                    for t in range(2):
                        a = 296 + 16 * c + 8 * t
                        x3 = qk[:, c, t, :].rearrange("p (h n) -> p h n", h=8)
                        TT(x3, x3, per(small[:, a:a + 8], 64, 8), MUL).then_inc(S["vec_step"], 1)
                        vec.wait_ge(S["vec_step"], next(vec_steps))
                        TT(rot[:, 0], x3, rep(tabs[:, c, 0, t, :], 8), MUL).then_inc(S["vec_step"], 1)
                        vec.wait_ge(S["vec_step"], next(vec_steps))
                        TT(rot[:, 1, :, 0:32], x3[:, :, 32:64], rep(tabs[:, c, 1, t, 0:32], 8), MUL).then_inc(S["vec_step"], 1)
                        vec.wait_ge(S["vec_step"], next(vec_steps))
                        TT(rot[:, 1, :, 32:64], x3[:, :, 0:32], rep(tabs[:, c, 1, t, 32:64], 8), MUL).then_inc(S["vec_step"], 1)
                        vec.wait_ge(S["vec_step"], next(vec_steps))
                        TT(qkr[:, c, t, :].rearrange("p (h n) -> p h n", h=8), rot[:, 0], rot[:, 1], ADD).then_inc(S["qk_rot"], 1)
                        vec.wait_ge(S["qk_rot"], 4 * l + 2 * c + t + 1)
                vec.wait_ge(*when_full(("gate", l)))
                b = bank_of(("gate", l))
                vec.wait_ge(*when_empty(("u", l, 3)))
                for j in range(2):
                    ps3 = b[:, SEQ * j:SEQ * j + SEQ].rearrange("p (t n) -> p t n", t=2)
                    ins = STT(out=vtmp[:, SEQ * j:SEQ * j + SEQ].rearrange("p (t n) -> p t n", t=2), in0=ps3, scalar=k2(l, "v_g", 1, j), in1=rep(bs_b[:, j, :], 2),
                              op0=MUL, op1=ADD)
                ins.then_inc(*emptying(("gate", l)))
                vec.wait_ge(*when_empty(("gate", l)))
                TT(mixT[:, 2:4, :].rearrange("p a b -> p (a b)"), vtmp, ug.rearrange("p a b -> p (a b)"), MUL).then_inc(S["mix_gmlp"], 1)
                vec.wait_ge(S["lam_exp"], l + 1)
                TT(small[:, 364:365], small[:, 363:364], small[:, 362:363], SUB).then_inc(S["vec_step"], 1)
                vec.wait_ge(S["vec_step"], next(vec_steps))
                TS(small[:, 364:365], small[:, 364:365], -lam_init, None, ADD).then_inc(S["vec_step"], 1)
                vec.wait_ge(S["vec_step"], next(vec_steps))

                def attention_out(t):
                    key = ("do", l, t)
                    vec.wait_ge(*when_full(key))
                    b = bank_of(key)
                    o = o2[:, t, :].rearrange("p (h n) -> p h n", h=4)
                    TC(o2[:, t, :], b[:, :]).then_inc(*emptying(key))
                    vec.wait_ge(*when_empty(key))
                    TT(rot[:, 0].rearrange("p a b -> p (a b)"), o2[:, t, :], o2[:, t, :], MUL).then_inc(S["vec_step"], 1)
                    vec.wait_ge(S["vec_step"], next(vec_steps))
                    a = 344 + 4 * t
                    V.tensor_reduce(small[:, a:a + 4], rot[:, 0].rearrange("p a b -> p (a b)").rearrange("p (h n) -> p h n", h=4), AX_X, ADD).then_inc(S["vec_step"], 1)
                    vec.wait_ge(S["vec_step"], next(vec_steps))
                    TS(small[:, a:a + 4], small[:, a:a + 4], 1.0 / 128, EPS, MUL, ADD).then_inc(S["d_var"], 1)
                    vec.wait_ge(S["d_rstd"], 2 * l + t + 1)
                    TT(o, o, per(small[:, 352 + 4 * t:356 + 4 * t], 128, 4), MUL).then_inc(S["d_hat"], 1)
                for i in range(8 + 1):
                    if i < 8:
                        keys, q = P * (i // 4 + 1), 2 * (i % 2)
                        for c in range(2):
                            vec.wait_ge(*when_full(("ds", l, i, c)))
                            b = bank_of(("ds", l, i, c))
                            V.tensor_reduce(small[:, 328 + q + c:329 + q + c], b[:, 0:keys], AX_X, MAX, negate=True).then_inc(S["vec_step"], 1)
                            vec.wait_ge(S["vec_step"], next(vec_steps))
                        TS(small[:, 332 + q:334 + q], small[:, 328 + q:330 + q], 0.125, None, MUL).then_inc(S["d_bias"], 1)
                    if i >= 1:
                        n = i - 1
                        keys, q = P * (n // 4 + 1), 2 * (n % 2)
                        vec.wait_ge(*when_empty(("ds", l, n, 0)))
                        vec.wait_ge(*when_empty(("ds", l, n, 1)))
                        V.reciprocal(small[:, 340 + q:342 + q], small[:, 336 + q:338 + q]).then_inc(S["vec_step"], 1)
                        vec.wait_ge(S["vec_step"], next(vec_steps))
                        TT(small[:, 341 + q:342 + q], small[:, 341 + q:342 + q], small[:, 364:365], MUL).then_inc(S["vec_step"], 1)
                        vec.wait_ge(S["vec_step"], next(vec_steps))
                        p0, p1 = prob2[:, n % 2, 0:keys], prob2[:, n % 2, SEQ:SEQ + keys]
                        TS(p1, p1, small[:, 341 + q:342 + q], None, MUL).then_inc(S["vec_step"], 1)
                        vec.wait_ge(S["vec_step"], next(vec_steps))
                        STT(out=p0, in0=p0, scalar=small[:, 340 + q:341 + q], in1=p1, op0=MUL, op1=ADD).then_inc(S["d_w"], 1)
                attention_out(0)
                attention_out(1)
                vec.wait_ge(*when_empty(("bT", l)))
                for s in range(ST):
                    vec.wait_ge(*when_full(("bu", l, s)))
                    b = bank_of(("bu", l, s))
                    cs, sn = csc[:, s, 0:2, :].rearrange("p a b -> p (a b)"), csc[:, s, 1:3, :].rearrange("p a b -> p (a b)")
                    TT(m1, b[:, :], cs, MUL).then_inc(S["vec_step"], 1)
                    vec.wait_ge(S["vec_step"], next(vec_steps))
                    TT(m2, b[:, :], sn, MUL).then_inc(*emptying(("bu", l, s)))
                    vec.wait_ge(*when_empty(("bu", l, s)))
                    TT(xr[:, 0:SEQ], m1[:, 0:SEQ], m1[:, SEQ:512], ADD).then_inc(S["vec_step"], 1)
                    vec.wait_ge(S["vec_step"], next(vec_steps))
                    TT(xr[:, SEQ:512], m2[:, SEQ:512], m2[:, 0:SEQ], SUB).then_inc(S["vec_step"], 1)
                    vec.wait_ge(S["vec_step"], next(vec_steps))
                    if s >= 2:
                        vec.wait_ge(S["rotated"], 2 * (ST * l + s - 1))
                    for c in range(2):
                        ins = V.tensor_tensor_scan(gs[:, s % 2, SEQ * c:SEQ * c + SEQ], small[:, 440 + s:441 + s].to_broadcast([P, SEQ]),
                                                   xr[:, SEQ * c:SEQ * c + SEQ], 0.0, MUL, ADD)
                    ins.then_inc(S["scanned"], 1)
                vec.wait_ge(*when_full(("ssm_y", l)))
                b = bank_of(("ssm_y", l))
                for m in range(2):
                    ins = STT(out=m1[:, SEQ * m:SEQ * m + SEQ], in0=uT[:, m, :], scalar=k2(l, "ssm_d", 1, m), in1=b[:, SEQ * m:SEQ * m + SEQ], op0=MUL, op1=ADD)
                ins.then_inc(*emptying(("ssm_y", l)))
                vec.wait_ge(*when_empty(("ssm_y", l)))
                TT(m2, m1, m1, MUL).then_inc(S["vec_step"], 1)
                vec.wait_ge(S["vec_step"], next(vec_steps))
                TS(m2, m2, 0.044715, 1.0, MUL, ADD).then_inc(S["vec_step"], 1)
                vec.wait_ge(S["vec_step"], next(vec_steps))
                TT(m2, m2, m1, MUL).then_inc(S["y_cubic"], 1)
                vec.wait_ge(S["y_tanh"], l + 1)
                STT(out=m2, in0=m2, scalar=1.0, in1=m1, op0=ADD, op1=MUL).then_inc(S["vec_step"], 1)
                vec.wait_ge(S["vec_step"], next(vec_steps))
                TS(mixT[:, 0:2, :].rearrange("p a b -> p (a b)"), m2, 0.5, None, MUL).then_inc(S["y_gelu"], 1)
                vec.wait_ge(*when_empty(("glu", l)))
                vec.wait_ge(S["y_gelu"], l + 1)
                STT(out=m1, in0=m1, scalar=1.0, in1=mixT[:, 0:2, :].rearrange("p a b -> p (a b)"), op0=ADD, op1=MUL).then_inc(S["vec_step"], 1)
                vec.wait_ge(S["vec_step"], next(vec_steps))
                TS(mixT[:, 0:2, :].rearrange("p a b -> p (a b)"), m1, 0.5, None, MUL).then_inc(S["mix_ssm"], 1)
                for j in range(2):
                    for t in range(2):
                        vec.wait_ge(*when_full(("out2", l, j, t)))
                        b = bank_of(("out2", l, j, t))
                        x = xc[:, t, 512 * j:512 * j + 512]
                        TT(x, x, b[:, :], ADD).then_inc(*emptying(("out2", l, j, t)))
                        vec.wait_ge(*when_empty(("out2", l, j, t)))
                norm(2 * l + 1)
                channels_odd("xf", "ffn_g")

                def gate_part(m):
                    vec.wait_ge(S["gelu_tanh"], FB * l + m + 1)
                    p = m % 2
                    STT(out=ge[:, p, 1, :], in0=ge[:, p, 1, :], scalar=1.0, in1=cv[:, p, 0, :], op0=ADD, op1=MUL).then_inc(S["vec_step"], 1)
                    vec.wait_ge(S["vec_step"], next(vec_steps))
                    STT(out=actT[:, m, :], in0=ge[:, p, 1, :], scalar=0.5, in1=cv[:, p, 1, :], op0=MUL, op1=MUL).then_inc(S["act_T"], 1)
                for m in range(FB):
                    p = m % 2
                    vec.wait_ge(*when_empty(("up", l, m)))
                    for tap in (1, 0):
                        for half in range(2):
                            ins = STT(out=cv[:, p, half, :], in0=hp[:, p, half, tap:tap + SEQ], scalar=k2(l, "conv01", 1, 44 * tap + FB * half + m), in1=cv[:, p, half, :],
                                      op0=MUL, op1=ADD)
                        ins.then_inc(S["vec_step"], 1)
                        vec.wait_ge(S["vec_step"], next(vec_steps))
                    TT(ge[:, p, 0, :], cv[:, p, 0, :], cv[:, p, 0, :], MUL).then_inc(S["vec_step"], 1)
                    vec.wait_ge(S["vec_step"], next(vec_steps))
                    TS(ge[:, p, 0, :], ge[:, p, 0, :], 0.044715, 1.0, MUL, ADD).then_inc(S["vec_step"], 1)
                    vec.wait_ge(S["vec_step"], next(vec_steps))
                    TT(ge[:, p, 0, :], ge[:, p, 0, :], cv[:, p, 0, :], MUL).then_inc(S["gelu_in"], 1)
                    if m:
                        gate_part(m - 1)
                gate_part(FB - 1)
                for q in range(4):
                    t, j = q // 2, q % 2
                    vec.wait_ge(*when_full(("down", l, q)))
                    b = bank_of(("down", l, q))
                    x = xc[:, t, 512 * j:512 * j + 512]
                    TT(x, x, b[:, :], ADD).then_inc(*emptying(("down", l, q)))
                    vec.wait_ge(*when_empty(("down", l, q)))

        @block.gpsimd
        def _(pool):
            G = nc.gpsimd


            def rsqrt(out_, in_):
                rows, n = in_.shape
                return G.tensor_tensor(out_, in_, C("negpow", 1, rows).to_broadcast([rows, n]), POW)
            G.memset(ubuf[:, :, :, 0], 0.0)
            G.memset(ubuf[:, :, :, SEQ + 1], 0.0).then_inc(S["pads"], 1)
            pool.wait_ge(S["consts"], 16)
            pool.wait_ge(S["levels"], 16)
            G.tensor_copy(lev[:, :], lev_f).then_inc(S["levels"], 1)
            pool.wait_ge(S["var_1"], 1)
            rsqrt(small[:, 116:120], small[:, 116:120]).then_inc(S["rstd_1"], 1)
            pool.wait_ge(*when_empty("lat_ssq"))
            rsqrt(small[:, 126:132], small[:, 120:126]).then_inc(S["rstd_lat"], 1)
            pool.wait_ge(*when_empty("kk_len"))
            rsqrt(rn[0:8, :], rn[0:8, :]).then_inc(S["kk_rn"], 1)
            pool.wait_ge(S["y_var"], 2)
            rsqrt(small[:, 208:224], small[:, 208:224]).then_inc(S["y_rstd"], 1)
            pool.wait_ge(S["y_rstd"], 1)
            G.memset(small[:, 510:511], 0.0).then_inc(S["y_rstd"], 1)
            pool.wait_ge(S["var_f"], 1)
            rsqrt(small[:, 242:244], small[:, 240:242]).then_inc(S["rstd_f"], 1)

            def load_params(l):
                def go(dst, src):
                    pool.dma_start(dst, src).then_inc(S["p2_load"], 16)
                    count[0] += 1

                def spread(src, rows, n):
                    return src.rearrange("(o n) -> o n", o=1).to_broadcast([rows, n])
                count = [0]
                for c, part in enumerate(("re", "im")):
                    go(b_rows[:, c], w[f"ssm_b_{part}_2"][l].rearrange("(t g) p c -> (g p) t c", g=2))
                    for dup in range(2):
                        go(c_rows[:, c, :, 64 * dup:64 * dup + 64], w[f"ssm_c_{part}_2"][l].rearrange("(j g) h p -> (g h) j p", j=2))
                go(ws, w["gmlp_w_s_2"][l].rearrange("h i j -> i h j"))
                for h in range(4):
                    go(bs_b[64 * (h % 2):64 * (h % 2) + 64, h // 2, :], spread(w["gmlp_b_s_2"][l, h], 64, P))
                for c, name in enumerate(("q_norm_g_2", "k_norm_g_2")):
                    g = w[name][l]
                    go(gains[:, 2 * c, :], spread(g, P, 64))
                    go(gains[:, 2 * c + 1, 0:32], spread(g[32:64], P, 32))
                    go(gains[:, 2 * c + 1, 32:64], spread(g[0:32], P, 32))
                for q, name in enumerate(("lambda_q1_2", "lambda_q2_2", "lambda_k1_2", "lambda_k2_2")):
                    go(lam_b[:, q, :], spread(w[name][l], P, 64))
                go(ldt_b, spread(w["ssm_log_dt_2"][l], P, 16))
                go(wglu, w["ssm_w_glu_2"][l].rearrange("(k p) n -> p k n", p=P))
                assert count[0] == P2_DMAS, count
            pool.wait_ge(S["x1"], 2)
            load_params(0)
            for l in range(DEPTH):
                pool.wait_ge(S["var_a"], 2 * l + 1)
                rsqrt(small[:, 258:260], small[:, 256:258]).then_inc(S["rstd_a"], 1)
                pool.wait_ge(S["u_theta"], l + 1)
                G.tensor_tensor(ang, small[:, 448:456].rearrange("p (c o) -> p c o", o=1).to_broadcast([P, ST, SEQ]),
                                     C("time", SEQ).rearrange("p (o n) -> p o n", o=1).to_broadcast([P, ST, SEQ]), MUL).then_inc(S["angle_raw"], 1)
                pool.wait_ge(S["vg_var"], l + 1)
                rsqrt(small[:, 262:264], small[:, 260:262]).then_inc(S["vg_rstd"], 1)
                pool.wait_ge(S["qk_var"], l + 1)
                rsqrt(small[:, 296:328], small[:, 264:296]).then_inc(S["qk_rstd"], 1)
                for t in range(2):
                    pool.wait_ge(S["d_var"], 2 * l + t + 1)
                    rsqrt(small[:, 352 + 4 * t:356 + 4 * t], small[:, 344 + 4 * t:348 + 4 * t]).then_inc(S["d_rstd"], 1)
                for s in range(ST):
                    pool.wait_ge(S["scanned"], ST * l + s + 1)
                    if s >= 2:
                        pool.wait_ge(S["rotated_used"], (ST - 1) * l + s - 1)
                    g = gs[:, s % 2, :]
                    G.tensor_tensor(pr1[:, s % 2, :], g, csc[:, s, 0:2, :].rearrange("p a b -> p (a b)"), MUL).then_inc(S["rotated"], 1)
                    G.tensor_tensor(pr2[:, s % 2, :], g, csc[:, s, 1:3, :].rearrange("p a b -> p (a b)"), MUL).then_inc(S["rotated"], 1)
                pool.wait_ge(*when_empty(("out2", l, 1, 1)))
                pool.wait_ge(S["var_a"], 2 * l + 2)
                rsqrt(small[:, 258:260], small[:, 256:258]).then_inc(S["rstd_a"], 1)
                G.memset(hp[:, :, :, 0:2], 0.0).then_inc(S["hp_pads"], 1)
                if l + 1 < DEPTH:
                    load_params(l + 1)

        @block.sync
        def _(sp):
            for n, (name, parts) in enumerate(tiles):
                if replaces[n] is not None:
                    sem, value = released[replaces[n]]
                    sp.wait_ge(sem, value)
                elif slot_of[n] >= RING_1:
                    sp.wait_ge(S["x1"], 2)
                for (a, e), shape, src in parts:
                    dst = slot(n)[:, a:e]
                    if shape:
                        dst = dst.rearrange("p (k n) -> p k n", k=shape[0])
                    sp.dma_start(dst, src).then_inc(slot_full[slot_of[n]], 16)
            for q in range(4):
                sp.wait_ge(*when_empty(("down", DEPTH - 1, q)))
            sp.dma_start(out.rearrange("a (t p) d -> p (a t) d", p=P), xc[:, 0:2, :]).then_inc(S["out_done"], 16)
            sp.wait_ge(S["out_done"], 16)


NAMES = """x c ctx c_ctx ada_w ada_b norm_g w_in shift_mu rw_w0 rw_w2 rw_a0 rw_a2 rw_kk rw_ka rw_rk rw_lnx_g rw_lnx_b
 mla_q_norm_g mla_kv_norm_g mla_w_uq mla_w_ukv w_out final_g attn_norm_g_2 w_in_2 ssm_a_re_2 ssm_a_im_2 ssm_log_dt_2
 ssm_b_re_2 ssm_b_im_2 ssm_c_re_2 ssm_c_im_2 ssm_d_2 ssm_w_glu_2 ssm_b_glu_2 gmlp_v_g_2 gmlp_w_s_2 gmlp_b_s_2 q_norm_g_2
 k_norm_g_2 lambda_q1_2 lambda_k1_2 lambda_q2_2 lambda_k2_2 subln_g_2 w_out_2 ffn_norm_g_2 w_up_2 conv_w_2 conv_b_2 w_down_2""".split()


def kernel(**inputs):
    import concourse.bacc as bacc
    from concourse.bass_utils import run_bass_kernel_spmd

    nc = bacc.Bacc("TRN2", target_bir_lowering=False, num_devices=1)
    arrays = {n: np.ascontiguousarray(inputs[n]) for n in NAMES}
    floats, masks = shape_constants()
    arrays["constants"], arrays["level_masks"] = floats, masks
    aps = {n: nc.dram_tensor(f"in_{n}", a.shape, mybir.dt.from_np(a.dtype), kind="ExternalInput").ap() for n, a in arrays.items()}
    out = nc.dram_tensor("out_0", (1, SEQ, D), F32, kind="ExternalOutput").ap()
    build(nc, aps, aps["constants"], aps["level_masks"], out)
    r = run_bass_kernel_spmd(nc, [{f"in_{n}": a for n, a in arrays.items()}], core_ids=[0])
    return r.results[0]["out_0"]
```
